# Optimizing a Trainium2 kernel written in Bass

```python
import jax, jax.numpy as jnp
from jax import lax
import numpy as np

D_MODEL = 2048
BATCH = 1
SEQ = 512
DEPTH = 2
DEC_BATCH = 8
DEC_SEQ = 8
PAST_LEN = 1024
PAGE_SIZE = 128

N_A_LAYERS = DEPTH // 2
N_B_LAYERS = DEPTH - N_A_LAYERS
D_CONV = D_MODEL
CONV_WIDTH = 3
N_HEADS = 16
Q_LORA_RANK = 512
KV_LORA_RANK = 512
QK_NOPE_DIM = 128
QK_ROPE_DIM = 64
V_HEAD_DIM = 128
D_ATTN = N_HEADS * V_HEAD_DIM
SOFTMAX_SCALE = (QK_NOPE_DIM + QK_ROPE_DIM) ** -0.5
ROPE_THETA = 10000.0
RMS_EPS = 1e-6
Q_BLOCK = 128

kernel_name = "yoco_shortconv_mla_step"

def rms_norm(x, g):
    xf = x.astype(jnp.float32)
    y = xf * lax.rsqrt(jnp.mean(xf * xf, axis=-1, keepdims=True) + RMS_EPS)
    return (y * g.astype(jnp.float32)).astype(x.dtype)

def rope(x, pos):
    half = x.shape[-1] // 2
    inv_freq = ROPE_THETA ** (-jnp.arange(half, dtype=jnp.float32) / half)
    ang = pos.astype(jnp.float32)[:, None] * inv_freq[None, :]
    ang = ang.reshape((ang.shape[0],) + (1,) * (x.ndim - 3) + (half,))
    cos, sin = jnp.cos(ang).astype(x.dtype), jnp.sin(ang).astype(x.dtype)
    x1, x2 = x[..., :half], x[..., half:]
    return jnp.concatenate([x1 * cos - x2 * sin, x2 * cos + x1 * sin], axis=-1)

def modulated_prenorm(x, c, w_ada, b_ada, g_pre):
    mod = (jax.nn.silu(c) @ w_ada + b_ada)[:, None, :]
    shift, scale, gate = jnp.split(mod, 3, axis=-1)
    return rms_norm(x, g_pre) * (1 + scale) + shift, gate

def short_conv_mixer(h, conv_buf, w_in, w_conv, w_out):
    b_g, c_g, v, z = jnp.split(h @ w_in, 4, axis=-1)
    u = c_g * v
    padded = jnp.concatenate([conv_buf.astype(u.dtype), u], axis=1)
    t = h.shape[1]
    conv = w_conv[0] * padded[:, 0:t]
    for k in range(1, CONV_WIDTH):
        conv = conv + w_conv[k] * padded[:, k:k + t]
    y = b_g * conv * jax.nn.silu(z)
    return y @ w_out, padded[:, -(CONV_WIDTH - 1):]

def shared_latent_kv(x, pos, g_in, w_down, g_latent):
    ckv, kpe = jnp.split(rms_norm(x, g_in) @ w_down, [KV_LORA_RANK], axis=-1)
    return rms_norm(ckv, g_latent), rope(kpe, pos)

def mla_queries(h, pos, w_in, g_q, w_uq, w_kv_up):
    b, t = h.shape[:2]
    qa, z = jnp.split(h @ w_in, [Q_LORA_RANK], axis=-1)
    q = (rms_norm(qa, g_q) @ w_uq).reshape(b, t, N_HEADS, QK_NOPE_DIM + QK_ROPE_DIM)
    q_nope, q_pe = jnp.split(q, [QK_NOPE_DIM], axis=-1)
    q_pe = rope(q_pe, pos)
    q_lat = jnp.einsum('bthn,chn->bthc', q_nope, w_kv_up[..., :QK_NOPE_DIM])
    return q_lat, q_pe, z

def mla_output(o_lat, z, w_kv_up, w_out):
    b, t = o_lat.shape[:2]
    o = jnp.einsum('bthc,chv->bthv', o_lat, w_kv_up[..., QK_NOPE_DIM:]).reshape(b, t, D_ATTN)
    return (o * jax.nn.silu(z)) @ w_out

def prompt_latent_attention(q_lat, q_pe, ckv, kpe):
    b, s = q_lat.shape[:2]
    nb = s // Q_BLOCK
    ql = q_lat.reshape(b, nb, Q_BLOCK, N_HEADS, KV_LORA_RANK).transpose(1, 0, 2, 3, 4)
    qp = q_pe.reshape(b, nb, Q_BLOCK, N_HEADS, QK_ROPE_DIM).transpose(1, 0, 2, 3, 4)
    kpos = jnp.arange(s)

    def block(args):
        ql_b, qp_b, i = args
        sc = (jnp.einsum('bqhc,bkc->bhqk', ql_b, ckv)
              + jnp.einsum('bqhr,bkr->bhqk', qp_b, kpe)).astype(jnp.float32) * SOFTMAX_SCALE
        qpos = i * Q_BLOCK + jnp.arange(Q_BLOCK)
        sc = jnp.where(kpos[None, :] <= qpos[:, None], sc, -jnp.inf)
        p = jax.nn.softmax(sc, axis=-1).astype(ckv.dtype)
        return jnp.einsum('bhqk,bkc->bqhc', p, ckv)

    o = lax.map(block, (ql, qp, jnp.arange(nb)))
    return o.transpose(1, 0, 2, 3, 4).reshape(b, s, N_HEADS, KV_LORA_RANK)

def sample_latent_attention(q_lat, q_pe, ckv_new, kpe_new, cache_ckv, cache_kpe, page_table):
    bd, t = q_lat.shape[:2]
    past_ckv = cache_ckv[page_table].reshape(bd, -1, KV_LORA_RANK)
    past_kpe = cache_kpe[page_table].reshape(bd, -1, QK_ROPE_DIM)
    n_past = past_ckv.shape[1]
    s_past = (jnp.einsum('bqhc,bkc->bhqk', q_lat, past_ckv)
              + jnp.einsum('bqhr,bkr->bhqk', q_pe, past_kpe)).astype(jnp.float32) * SOFTMAX_SCALE
    s_new = (jnp.einsum('bqhc,bkc->bhqk', q_lat, ckv_new)
             + jnp.einsum('bqhr,bkr->bhqk', q_pe, kpe_new)).astype(jnp.float32) * SOFTMAX_SCALE
    causal = jnp.tril(jnp.ones((t, t), dtype=bool))
    s_new = jnp.where(causal, s_new, -jnp.inf)
    p = jax.nn.softmax(jnp.concatenate([s_past, s_new], axis=-1), axis=-1).astype(ckv_new.dtype)
    return (jnp.einsum('bhqk,bkc->bqhc', p[..., :n_past], past_ckv)
            + jnp.einsum('bhqk,bkc->bqhc', p[..., n_past:], ckv_new))

def setup_inputs(seed: int = 0) -> dict:
    key = jax.random.key(seed)
    ks = jax.random.split(key, 26)
    f32 = jnp.float32
    n_pages = PAST_LEN // PAGE_SIZE
    n_used = DEC_BATCH * n_pages
    n_pool = n_used + max(1, n_used // 4)
    nrm = lambda k, shape, s: jax.random.normal(k, shape, f32) * s
    page_table = jax.random.permutation(ks[0], n_pool)[:n_used].reshape(DEC_BATCH, n_pages).astype(jnp.int32)
    return {
        'x_prompt': nrm(ks[1], (BATCH, SEQ, D_MODEL), 1.0),
        'x_sample': nrm(ks[2], (DEC_BATCH, DEC_SEQ, D_MODEL), 1.0),
        'state_conv': nrm(ks[3], (N_A_LAYERS, DEC_BATCH, CONV_WIDTH - 1, D_CONV), 1.0),
        'cache_ckv': nrm(ks[4], (n_pool, PAGE_SIZE, KV_LORA_RANK), 1.0),
        'cache_kpe': nrm(ks[5], (n_pool, PAGE_SIZE, QK_ROPE_DIM), 1.0),
        'page_table': page_table,
        'c_prompt': nrm(ks[6], (BATCH, D_MODEL), 1.0),
        'c_sample': nrm(ks[7], (DEC_BATCH, D_MODEL), 1.0),
        'w_ada': nrm(ks[8], (DEPTH, D_MODEL, 3 * D_MODEL), 0.5 * D_MODEL ** -0.5),
        'b_ada': nrm(ks[9], (DEPTH, 3 * D_MODEL), 0.02),
        'g_pre': 1.0 + nrm(ks[10], (DEPTH, D_MODEL), 0.02),
        'g_post': 1.0 + nrm(ks[11], (DEPTH, D_MODEL), 0.02),
        'conv_w_in': nrm(ks[12], (N_A_LAYERS, D_MODEL, 4 * D_CONV), D_MODEL ** -0.5),
        'conv_w': nrm(ks[13], (N_A_LAYERS, CONV_WIDTH, D_CONV), CONV_WIDTH ** -0.5),
        'conv_w_out': nrm(ks[14], (N_A_LAYERS, D_CONV, D_MODEL), D_CONV ** -0.5),
        'kv_g_in': 1.0 + nrm(ks[15], (D_MODEL,), 0.02),
        'kv_w_down': nrm(ks[16], (D_MODEL, KV_LORA_RANK + QK_ROPE_DIM), D_MODEL ** -0.5),
        'kv_g_latent': 1.0 + nrm(ks[17], (KV_LORA_RANK,), 0.02),
        'kv_w_up': nrm(ks[18], (KV_LORA_RANK, N_HEADS, QK_NOPE_DIM + V_HEAD_DIM), KV_LORA_RANK ** -0.5),
        'mla_w_in': nrm(ks[19], (N_B_LAYERS, D_MODEL, Q_LORA_RANK + D_ATTN), D_MODEL ** -0.5),
        'mla_g_q': 1.0 + nrm(ks[20], (N_B_LAYERS, Q_LORA_RANK), 0.02),
        'mla_w_uq': nrm(ks[21], (N_B_LAYERS, Q_LORA_RANK, N_HEADS * (QK_NOPE_DIM + QK_ROPE_DIM)), Q_LORA_RANK ** -0.5),
        'mla_w_out': nrm(ks[22], (N_B_LAYERS, D_ATTN, D_MODEL), D_ATTN ** -0.5),
    }

def reference(x_prompt, x_sample, state_conv, cache_ckv, cache_kpe, page_table, c_prompt, c_sample,
              w_ada, b_ada, g_pre, g_post, conv_w_in, conv_w, conv_w_out,
              kv_g_in, kv_w_down, kv_g_latent, kv_w_up,
              mla_w_in, mla_g_q, mla_w_uq, mla_w_out):
    xp, xs = x_prompt, x_sample
    pos_p = jnp.arange(xp.shape[1])
    pos_s = PAST_LEN + jnp.arange(xs.shape[1])
    conv_p, conv_s = [], []
    ckv_p = kpe_p = ckv_s = kpe_s = None
    for l in range(DEPTH):
        if l == N_A_LAYERS:
            ckv_p, kpe_p = shared_latent_kv(xp, pos_p, kv_g_in, kv_w_down, kv_g_latent)
            ckv_s, kpe_s = shared_latent_kv(xs, pos_s, kv_g_in, kv_w_down, kv_g_latent)
        hp, gate_p = modulated_prenorm(xp, c_prompt, w_ada[l], b_ada[l], g_pre[l])
        hs, gate_s = modulated_prenorm(xs, c_sample, w_ada[l], b_ada[l], g_pre[l])
        if l < N_A_LAYERS:
            a = l
            zero_buf = jnp.zeros((xp.shape[0], CONV_WIDTH - 1, D_CONV), hp.dtype)
            op, buf_p = short_conv_mixer(hp, zero_buf, conv_w_in[a], conv_w[a], conv_w_out[a])
            os_, buf_s = short_conv_mixer(hs, state_conv[a], conv_w_in[a], conv_w[a], conv_w_out[a])
            conv_p.append(buf_p)
            conv_s.append(buf_s)
        else:
            b = l - N_A_LAYERS
            ql, qpe, z = mla_queries(hp, pos_p, mla_w_in[b], mla_g_q[b], mla_w_uq[b], kv_w_up)
            op = mla_output(prompt_latent_attention(ql, qpe, ckv_p, kpe_p), z, kv_w_up, mla_w_out[b])
            ql, qpe, z = mla_queries(hs, pos_s, mla_w_in[b], mla_g_q[b], mla_w_uq[b], kv_w_up)
            o_lat = sample_latent_attention(ql, qpe, ckv_s, kpe_s, cache_ckv, cache_kpe, page_table)
            os_ = mla_output(o_lat, z, kv_w_up, mla_w_out[b])
        xp = xp + gate_p * rms_norm(op, g_post[l])
        xs = xs + gate_s * rms_norm(os_, g_post[l])
    conv_state_p = jnp.stack(conv_p, axis=0)
    conv_state_s = jnp.stack(conv_s, axis=0)
    return (xp, xs, conv_state_p, conv_state_s, ckv_p, kpe_p, ckv_s, kpe_s)


_drawn_inputs = setup_inputs


def setup_inputs(seed=0):
    import zlib

    import numpy as np

    out = dict(_drawn_inputs(seed))
    spreads = {}
    factors = {'g_post': 7.071, 'kv_g_in': 2.749, 'kv_g_latent': 2.977, 'mla_g_q': 8.0}
    for name, (base, spread) in spreads.items():
        noise = np.random.default_rng([zlib.crc32(name.encode()), seed]).standard_normal(out[name].shape)
        drawn = base * np.exp(spread * noise) if base else spread * noise
        out[name] = __import__('jax').numpy.asarray(drawn.astype(out[name].dtype))
    for name, factor in factors.items():
        out[name] = (out[name] * factor).astype(out[name].dtype)
    return out
```

```python
from contextlib import ExitStack

import numpy as np

import concourse.bass as bass
from concourse import mybir

F32 = mybir.dt.float32
F32R = mybir.dt.float32r
I32 = mybir.dt.int32
ALU = mybir.AluOpType
ACT = mybir.ActivationFunctionType
AX = mybir.AxisListType

P = 128
D = 2048
KT = D // P
TP = 512
NB, NS = 8, 8
TS = NB * NS
T = TP + TS
HALF = T // 2
H = 16
R = 512
CT = R // P
NOPE, ROPE, VD = 128, 64, 128
RH = ROPE // 2
PAST, PAGE = 1024, 128
NPG = PAST // PAGE
POOL_PAGES = 80
SCALE = (NOPE + ROPE) ** -0.5
EPS = 1e-6
NEG = -1e30
G = 4
QT = TP // P
CH = 1024
NM = NB + 1
AB = 256
ADA0 = 2 * D // AB

W_CONV = 0
W_COUT = W_CONV + 4 * KT * 2
W_KV = W_COUT + KT * 2
W_MLA = W_KV + 2 * CT + 1
W_ROPE = W_MLA + 2 * (CT + H)
W_GRP = W_ROPE + H // G
W_OUT = W_GRP + 6 * (H // G)
W_END = W_OUT + KT * 2

PGT = CT * P + PAGE
PGW = PGT + R

_C = {}
_n = 0
for _name, _w in (("bada", 96), ("gpre", 2 * KT), ("gpost", 2 * KT), ("gin", KT), ("glat", CT), ("gq", CT),
                  ("cw", 3 * KT), ("c", KT * 32), ("state", KT * NB * 2), ("ident", P), ("ones", P),
                  ("sel", NM), ("mask", P), ("mask8", 8)):
    _C[_name] = (_n, _w)
    _n += _w
SMALL = _n


class Chunk:

    def __init__(self, c, k=0, i=None):
        self.c, self.k, self.i = c, k, i

    def __add__(self, d):
        return Chunk(self.c + d, self.k, self.i)

    def at(self, d=0):
        return self.c + d if self.i is None else self.i * self.k + (self.c + d)

    @property
    def slot(self):
        return self.c % 2

    def turns(self):
        return self.c // 2 + 1 if self.i is None else self.i * (self.k // 2) + (self.c // 2 + 1)


def build(nc, wstream, adastream, x_in, small_in, cos_in, sin_in, pages, ptab, wk_in, wv_in,
          y_out, cst_out, ckv_out, kpe_out, x1_park):
    with ExitStack() as ctx:
        base = 16512
        arena_floats = 53200
        ctx.enter_context(nc.sbuf_tensor("arena", [P, arena_floats], F32))
        top = [0]

        def at(name, off, shape, dt=F32):
            n = int(np.prod(shape[1:]))
            assert off + n <= arena_floats, (name, off + n)
            return nc.alloc_sbuf_tensor_at(name, shape, dt, offset=base + 4 * off)

        def place(n):
            off = top[0]
            top[0] += (n + 7) // 8 * 8
            assert top[0] <= arena_floats, top[0]
            return off

        def sem(name):
            return ctx.enter_context(nc.semaphore(name))

        xo = place(KT * T)
        X = at("x_residual", xo, [P, KT * T])
        QA = at("q_latent", xo, [P, CT * T])
        PT = at("probs_t", xo, [P, 10 * P])
        QPE = at("q_rope_group", xo + 1280, [P, 2 * TP])
        KTT = at("k_nope_t", xo + 2304, [P, G * TP])
        QNH = at("q_latent_hi", xo + 4608, [P, CT * T], F32R)
        QNL = at("q_latent_lo", xo + 6912, [P, CT * T], F32R)
        OLS = at("sample_out_latent", xo, [P, R])
        CKN = at("new_latent", xo + 512, [NS, R])
        B1 = at("tiles", place(KT * T), [P, KT * T])
        WR = at("w_raw", place(2 * CH), [P, 2, CH])
        WH = at("w_hi", place(2 * CH), [P, 2, CH], F32R)
        WL = at("w_lo", place(2 * CH), [P, 2, CH], F32R)
        po = place(2 * KT * T)
        OH = at("operand_hi", po, [P, KT * T], F32R)
        OL = at("operand_lo", po + KT * T, [P, KT * T], F32R)
        ADA_FIRST = at("ada_first_ring", po, [P, 8, CH])
        CKH = at("latent_hi", po, [P, CT * TP], F32R)
        CKL = at("latent_lo", po + 2048, [P, CT * TP], F32R)
        QPA = at("q_rope_all", po + 4096, [P, (H // 2) * TP])
        QN = at("q_nope", po + 8192, [P, G, T])
        V = at("values", po + 10496, [P, QT, G * VD])
        QLAT = at("q_lat", po + 12544, [P, CT, NB, P])
        QPS = at("q_rope_sample", po + 16640, [ROPE, NB, H, NS])
        PG = at("page_t", po, [P, NPG + 1, PGT])
        NAT = at("page_latent", po + 5760, [P, NPG, R])
        PTS = at("probs_t_sample", po + 9856, [P, NPG * P])
        PTN = at("probs_t_new", po + 10880, [NS, P])
        QS = at("q_batch", po + 11008, [P, CT * P + P])
        WV = at("wv_ring", po, [P, 2, CT * VD])
        ao = place(4 * CH)
        ADA_RING = at("ada_ring", ao, [P, 4, CH])
        COS = at("cos", ao, [P, T])
        SIN = at("sin", ao + T, [P, T])
        WK = at("wk_ring", ao, [P, 2, CT * P])
        CKV = at("latent", ao + 2 * T, [P, CT * T])
        KPE = at("k_rope", ao + 2 * T + CT * T, [P, T])
        MOD = at("mod", place(96 * NM), [P, 96, NM])
        SM = at("small", place(SMALL), [P, SMALL])
        AT = at("mod_scale", place(KT * NM), [P, KT, NM])
        CST = at("conv_state", place(KT * 18), [P, KT * 18])
        PART = at("ada_part", place(AB), [P, AB])
        MX = at("row_stats", place(24), [P, 24])
        PTB = at("page_ids", place(NB * NPG), [1, NB * NPG], I32)
        R0 = at("rstd0", place(T), [P, T])
        uo = place(TP + 8 + NB * (NS + 2))
        UP = at("u_prompt", uo, [P, TP + 2])
        US = at("u_sample", uo + TP + 8, [P, NB, NS + 2])
        R1 = at("rstd1", uo, [P, T])
        to = place(3 * T)
        T1 = at("tmp1", to, [P, T])
        T2 = at("tmp2", to + T, [P, T])
        ACC = at("acc", to + 2 * T, [P, T])
        PR = at("probs", to, [P, 10 * P])
        PRS = at("probs_sample", to, [P, PAST + NS])
        RS = [R0, R1]
        TT = [T1, T2]
        PS = ctx.enter_context(nc.psum_tensor("ps", [P, 8, 512], F32))

        def small(name, lo=0, n=None):
            o, w = _C[name]
            return SM[:, o + lo:o + (w if n is None else lo + n)]

        ident = small("ident")

        def pair(p, rows=P):
            return PS[0:rows, 2 * p:2 * p + 2, 0:HALF]

        def halves(ap):
            return ap.rearrange("p (a n) -> p a n", a=2)

        def toks(ap):
            return ap.rearrange("p (b t) -> p b t", b=NB)

        raw_landed = [sem(f"raw_landed{i}") for i in range(2)]
        w_hi_ready, w_lo_ready, w_used = sem("w_hi_ready"), sem("w_lo_ready"), sem("w_used")
        small_landed, x_landed = sem("small_landed"), [sem(f"x_landed{i}") for i in range(4)]
        rope_landed, ptab_landed = sem("rope_landed"), sem("ptab_landed")
        ada0_landed = [sem(f"ada0_landed{i}") for i in range(8)]
        ada_landed = [sem(f"ada_landed{i}") for i in range(4)]
        ada_used, ada_part, ada_sel, mod_done = sem("ada_used"), sem("ada_part"), sem("ada_sel"), sem("mod_done")
        silu_c, stat_done = sem("silu_c"), sem("stat_done")
        var_ready, root_ready = sem("var_ready"), sem("root_ready")
        xsq_ready, xsq_used = [sem(f"xsq_ready{i}") for i in range(2)], [sem(f"xsq_used{i}") for i in range(2)]
        h_raw, h_hi, h_ready = sem("h_raw"), sem("h_hi"), sem("h_ready")
        c_ready, u_done, z_ready, gate_done = sem("c_ready"), sem("u_done"), sem("z_ready"), sem("gate_done")
        y_hi, y_ready = sem("y_hi"), sem("y_ready")
        co = {k: [sem(f"co_{k}{i}") for i in range(2)] for k in ("sq", "sq_used", "evac")}
        x1_ready, x1sq, x1sq_used = sem("x1_ready"), [sem(f"x1sq{i}") for i in range(2)], [sem(f"x1sq_used{i}") for i in range(2)]
        xg_hi, xg_ready, x_parked = sem("xg_hi"), sem("xg_ready"), sem("x_parked")
        kv_evac, kv_sq, kv_sq_used = sem("kv_evac"), sem("kv_sq"), sem("kv_sq_used")
        h1_raw, h1_hi, h1_ready = sem("h1_raw"), sem("h1_hi"), sem("h1_ready")
        ckv_ready, kpe_ready = sem("ckv_ready"), sem("kpe_ready")
        qa_sq, qa_sq_used, qa_evac = ([sem(f"{k}{i}") for i in range(2)] for k in ("qa_sq", "qa_sq_used", "qa_evac"))
        z1_evac = [sem(f"z1_evac{i}") for i in range(2)]
        qn_raw, qn_hi, qn_ready = sem("qn_raw"), sem("qn_hi"), sem("qn_ready")
        rope_evac, qr_ready, ck_hi, ck_ready = sem("rope_evac"), sem("qr_ready"), sem("ck_hi"), sem("ck_ready")
        wk_landed = [sem(f"wk_landed{i}") for i in range(2)]
        k_evac, v_evac, q_evac, qpe_ready = sem("k_evac"), sem("v_evac"), sem("q_evac"), sem("qpe_ready")
        qlat_done, qlat_evac = sem("qlat_done"), sem("qlat_evac")
        score_done, bias_ready, exp_done, p_ready = sem("score_done"), sem("bias_ready"), sem("exp_done"), sem("p_ready")
        tr_done, ptv_evac, pta_evac, pv_done, o_done = (sem(n) for n in ("tr_done", "ptv_evac", "pta_evac", "pv_done", "o_done"))
        pgt_landed, nat_landed = sem("pgt_landed"), sem("nat_landed")
        sq_ready, sqk_done, new_done, new_evac = sem("sq_ready"), sem("sqk_done"), sem("new_done"), sem("new_evac")
        s_bias, s_exp, s_norm = sem("s_bias"), sem("s_exp"), sem("s_norm")
        str_done, spt_v, spt_a, spv_done, ols_ready, olt_done, olt_evac = (
            sem(n) for n in ("str_done", "spt_v", "spt_a", "spv_done", "ols_ready", "olt_done", "olt_evac"))
        wv_landed = [sem(f"wv_landed{i}") for i in range(2)]
        so_done, so_evac = sem("so_done"), sem("so_evac")
        o_hi, o_ready = sem("o_hi"), sem("o_ready")
        wo = {k: [sem(f"wo_{k}{i}") for i in range(2)] for k in ("sq", "sq_used", "evac")}
        x1_back, yout_ready = sem("x1_back"), sem("yout_ready")
        dve_step = sem("dve_step")
        stored = sem("stored")

        block = ctx.enter_context(nc.Block())

        @block.sync
        def _(sp):
            def load_w(n):
                if n.i is not None or n.c >= 2:
                    sp.wait_ge(w_lo_ready, n.at(-1))
                src = wstream[bass.ds(n.at(), 1), :, :].rearrange("a p n -> p (a n)")
                sp.dma_start(WR[:, n.slot, :], src).then_inc(raw_landed[n.slot], 16)

            def load_ada(blk, j, dst, landed):
                src = adastream[bass.ds(blk, 1), bass.ds(j, 1), :, :].rearrange("a b p n -> p (a b n)")
                sp.dma_start(dst, src).then_inc(landed, 16)

            sp.dma_start(SM[:, :], small_in).then_inc(small_landed, 16)
            for q in range(4):
                w = KT * T // 4
                sp.dma_start(X[:, q * w:(q + 1) * w], x_in[:, q * w:(q + 1) * w]).then_inc(x_landed[q], 16)
            sp.dma_start(PTB[:, :], ptab).then_inc(ptab_landed, 16)
            load_w(Chunk(0))
            load_w(Chunk(1))
            for q in range(2):
                for j in range(4):
                    load_ada(q, j, ADA_FIRST[:, 4 * q + j, :], ada0_landed[4 * q + j])
            with sp.Fori(1, ADA0 // 2) as i:
                for q in range(2):
                    for j in range(4):
                        sp.wait_ge(ada_used, i * 8 + (4 * q + j + 1 - 8))
                        load_ada(i * 2 + q, j, ADA_FIRST[:, 4 * q + j, :], ada0_landed[4 * q + j])
            for j in range(4):
                load_ada(ADA0, j, ADA_RING[:, j, :], ada_landed[j])
            def conv_loads(m, n, last):
                for k in range(8):
                    load_w(n + k)
                    q, j = k // 4, k % 4
                    if q == 0 or not last:
                        sp.wait_ge(ada_used, m * 8 + (4 * ADA0 + 4 * q + j + 1))
                        load_ada(m * 2 + (ADA0 + 1 + q), j, ADA_RING[:, j, :], ada_landed[j])

            with sp.Fori(0, KT - 1) as m:
                conv_loads(m, Chunk(2, 8, m), False)
            conv_loads(KT - 1, Chunk(2 + 8 * (KT - 1)), True)
            sp.wait_ge(ada_used, 4 * 48)
            sp.dma_start(COS[:, :], cos_in).then_inc(rope_landed, 16)
            sp.dma_start(SIN[:, :], sin_in).then_inc(rope_landed, 16)
            sp.wait_ge(gate_done, KT)
            sp.dma_start(cst_out, CST[:, :]).then_inc(stored, 16)
            with sp.Fori(0, (W_KV - W_COUT) // 2) as i:
                for k in range(2):
                    load_w(Chunk(W_COUT + 2 + k, 2, i))
            for n in range(W_KV + 2, W_MLA + 2):
                load_w(Chunk(n))
                if n == W_KV + 3:
                    sp.wait_ge(x1_ready, KT)
                    sp.dma_start(x1_park, X[:, :]).then_inc(x_parked, 16)
            with sp.Fori(0, (W_ROPE - W_MLA) // 2) as i:
                for k in range(2):
                    load_w(Chunk(W_MLA + 2 + k, 2, i))
            for n in range(W_ROPE + 2, W_GRP + 2):
                load_w(Chunk(n))
            sp.wait_ge(ckv_ready, CT)
            sp.dma_start(ckv_out, CKV[:, :]).then_inc(stored, 16)
            sp.wait_ge(kpe_ready, 1)
            sp.dma_start(kpe_out, KPE[0:ROPE, :]).then_inc(stored, 16)

            def load_wk(h, s):
                sp.dma_start(WK[:, s, :], wk_in[bass.ds(h, 1), :, :].rearrange("a p n -> p (a n)")).then_inc(wk_landed[s], 16)

            sp.wait_ge(rope_evac, H // G)
            load_wk(0, 0)
            load_wk(1, 1)

            def group_loads(g, n, last):
                for k in range(6):
                    load_w(n + k)
                for j in range(2 if last else G):
                    sp.wait_ge(qlat_done, g * G + (j + 1))
                    load_wk(g * G + (j + 2), j % 2)

            with sp.Fori(0, H // G - 1) as g:
                group_loads(g, Chunk(W_GRP + 2, 6, g), False)
            group_loads(H // G - 1, Chunk(W_GRP + 2 + 6 * (H // G - 1)), True)
            sp.wait_ge(ptab_landed, 16)
            sp.wait_ge(pv_done, H)
            def load_pages(b, dst, lo, hi, landed, used):
                for j in range(NPG):
                    pid = sp.value_load(PTB[0:1, bass.ds(b * NPG + j, 1)], min_val=0, max_val=POOL_PAGES - 1)
                    if j == 0 and used is not None:
                        sp.wait_ge(*used)
                    sp.dma_start(dst[:, j, :], pages[bass.ds(pid, 1), :, lo:hi].rearrange("a p n -> p (a n)")).then_inc(landed, 16)

            def load_keys(b, used=None):
                load_pages(b, PG, 0, PGT, pgt_landed, used)

            def load_latents(b, used=None):
                load_pages(b, NAT, PGT, PGW, nat_landed, used)

            load_keys(0)
            load_latents(0)
            load_keys(1, (sqk_done, 1))
            with sp.Fori(1, NB - 1) as b:
                load_keys(b + 1, (sqk_done, b + 1))
                load_latents(b, (spv_done, b))
            load_latents(NB - 1, (spv_done, NB - 1))

            def load_wv(h, s):
                sp.dma_start(WV[:, s, :], wv_in[bass.ds(h, 1), :, :].rearrange("a p n -> p (a n)")).then_inc(wv_landed[s], 16)

            sp.wait_ge(new_done, NB)
            load_wv(0, 0)
            load_wv(1, 1)
            with sp.Fori(1, H // 2) as i:
                for s in range(2):
                    sp.wait_ge(so_done, i * 2 + (s - 1))
                    load_wv(i * 2 + s, s)
            sp.wait_ge(olt_evac, NB)
            sp.dma_start(X[:, :], x1_park).then_inc(x1_back, 16)
            with sp.Fori(0, (W_END - W_OUT - 2) // 2) as i:
                for k in range(2):
                    load_w(Chunk(W_OUT + 2 + k, 2, i))
            for kt in range(KT):
                sp.wait_ge(yout_ready, kt + 1)
                sp.dma_start(y_out[:, kt * T:(kt + 1) * T], X[:, kt * T:(kt + 1) * T]).then_inc(stored, 16)
            sp.wait_ge(stored, 16 * (3 + KT))

        @block.gpsimd
        def _(pool):
            def rest(n):
                pool.wait_ge(w_hi_ready, n.at(1))
                pool.tensor_tensor(WL[:, n.slot, :], WR[:, n.slot, :], WH[:, n.slot, :].bitcast(F32),
                                   ALU.subtract).then_inc(w_lo_ready, 1)

            with pool.Fori(0, W_END // 2) as i:
                rest(Chunk(0, 2, i))
                rest(Chunk(1, 2, i))
            rest(Chunk(W_END - 1))

        @block.tensor
        def _(pe):
            def tile(n, p, ready=None, each=None, hi=OH, lo=OL, kts=KT, cols=P, split=2):
                per = kts // split
                last = None
                for q in range(split):
                    c = n + q
                    pe.wait_ge(w_hi_ready, c.at(1))
                    for kk in range(per):
                        k = q * per + kk
                        if each:
                            each(k)
                        if ready:
                            pe.wait_ge(ready, k + 1)
                        for a in range(2):
                            for x in (hi, lo):
                                pe.matmul(PS[0:cols, 2 * p + a, 0:HALF], WH[:, c.slot, kk * cols:(kk + 1) * cols],
                                          x[:, k * T + a * HALF:k * T + (a + 1) * HALF],
                                          start=(k == 0 and x is hi), stop=False)
                    pe.wait_ge(w_lo_ready, c.at(1))
                    for kk in range(per):
                        k = q * per + kk
                        for a in range(2):
                            last = pe.matmul(PS[0:cols, 2 * p + a, 0:HALF], WL[:, c.slot, kk * cols:(kk + 1) * cols],
                                             hi[:, k * T + a * HALF:k * T + (a + 1) * HALF],
                                             start=False, stop=(k == kts - 1))
                    last.then_inc(w_used, 1)

            def ada_block(ring, slots, landed, turns, bank):
                for j in range(4):
                    pe.wait_ge(landed[j], turns * 16)
                    for g in range(4):
                        k = 4 * j + g
                        last = pe.matmul(PS[32 * g:32 * g + 32, bank, 0:AB], small("c", 32 * k, 32),
                                         ring[:, slots + j, g * AB:(g + 1) * AB],
                                         start=(j == 0), stop=(j == 3), skip_group_check=True)
                    last.then_inc(ada_used, 1)

            def ada_select(n, bank, before):
                pe.wait_ge(ada_part, n)
                if before is not None:
                    pe.wait_ge(mod_done, before)
                for q in range(2):
                    last = pe.matmul(PS[:, bank, q * NM:(q + 1) * NM], PART[:, q * P:(q + 1) * P], small("sel"),
                                     start=True, stop=True)
                last.then_inc(ada_sel, 1)

            def column_sums(added, n):
                for s in added:
                    pe.wait_ge(s, n)
                for a in range(2):
                    last = pe.matmul(PS[:, 6 + a, 0:HALF], small("ones"), ACC[:, a * HALF:(a + 1) * HALF],
                                     start=True, stop=True)
                last.then_inc(stat_done, 1)

            def add_squares(ready, used, k, n):
                pe.wait_ge(ready[k % 2], k // 2 + 1)
                for a in range(2):
                    last = pe.matmul(PS[:, 6 + a, 0:HALF], small("ones"), TT[k % 2][:, a * HALF:(a + 1) * HALF],
                                     start=(k == 0), stop=(k == n - 1), skip_group_check=True)
                last.then_inc(used[k % 2] if k < n - 1 else stat_done, 1)

            pe.wait_ge(small_landed, 16)
            for k in range(KT):
                add_squares(xsq_ready, xsq_used, k, KT)
            pe.wait_ge(silu_c, 1)
            with pe.Fori(0, ADA0 // 2) as i:
                for q in range(2):
                    ada_block(ADA_FIRST, 4 * q, ada0_landed[4 * q:4 * q + 4], i + 1, 4 + q)
                    ada_select(i * 2 + (q + 1), 2 + q, i * 2 + q)

            with pe.Fori(0, KT) as m:
                n = Chunk(W_CONV, 8, m)
                pe.wait_ge(z_ready, m)
                tile(n, 0, ready=h_ready)
                ada_block(ADA_RING, 0, ada_landed, m * 2 + 1, 4)
                pe.wait_ge(gate_done, m)
                tile(n + 2, 1)
                ada_select(m * 2 + (ADA0 + 1), 5, m * 2 + ADA0)
                pe.wait_ge(c_ready, m + 1)
                tile(n + 4, 0)
                ada_block(ADA_RING, 0, ada_landed, m * 2 + 2, 4)
                pe.wait_ge(u_done, m + 1)
                tile(n + 6, 1)
                ada_select(m * 2 + (ADA0 + 2), 5, m * 2 + (ADA0 + 1))

            def project_out(w0, ready, s):
                with pe.Fori(0, KT // 2) as i:
                    for j in range(2):
                        pe.wait_ge(s["evac"][j], i)
                        tile(Chunk(w0 + 2 * j, 4, i), j, ready=ready if j == 0 else None)
                column_sums(s["sq_used"], KT // 2)

            pe.wait_ge(z_ready, KT)
            pe.wait_ge(gate_done, KT)
            project_out(W_COUT, y_ready, co)

            pe.wait_ge(var_ready, 2)
            for t in range(CT):
                if t >= 2:
                    pe.wait_ge(kv_evac, t - 1)
                else:
                    pe.wait_ge(co["evac"][t], KT // 2)
                if t == 0:
                    tile(Chunk(W_KV), 0, ready=xg_ready, each=lambda k: add_squares(x1sq, x1sq_used, k, KT))
                else:
                    tile(Chunk(W_KV + 2 * t), t % 2)
            pe.wait_ge(kv_evac, CT - 1)
            tile(Chunk(W_KV + 2 * CT), 0, cols=ROPE, split=1)
            column_sums([kv_sq_used], CT)

            pe.wait_ge(kv_evac, CT + 1)
            with pe.Fori(0, CT // 2) as i:
                for j in range(2):
                    pe.wait_ge(qa_evac[j], i)
                    tile(Chunk(W_MLA + 2 * j, 4, i), j, ready=h1_ready if j == 0 else None)

            def gate_tiles(i, n):
                for j in range(2):
                    pe.wait_ge(z1_evac[j], i)
                    tile(n + 2 * j, j)

            for j in range(2):
                pe.wait_ge(qa_evac[j], CT // 2)
            gate_tiles(0, Chunk(W_MLA + 2 * CT))
            column_sums(qa_sq_used, CT // 2)
            with pe.Fori(1, H // 2) as i:
                gate_tiles(i, Chunk(W_MLA + 2 * CT, 4, i))
            for j in range(2):
                pe.wait_ge(z1_evac[j], H // 2)

            pe.wait_ge(qn_ready, CT)
            for g in range(H // G):
                n = Chunk(W_ROPE + g)
                if g:
                    pe.wait_ge(rope_evac, g)
                pe.wait_ge(w_hi_ready, n.at(1))
                for w in (WH, WL):
                    if w is WL:
                        pe.wait_ge(w_lo_ready, n.at(1))
                    for k in range(CT):
                        for p in range(2):
                            for a in range(2):
                                for x in (QNH, QNL) if w is WH else (QNH,):
                                    last = pe.matmul(PS[:, 2 * p + a, 0:HALF],
                                                     w[:, n.slot, k * 256 + p * P:k * 256 + (p + 1) * P],
                                                     x[:, k * T + a * HALF:k * T + (a + 1) * HALF],
                                                     start=(w is WH and k == 0 and x is QNH),
                                                     stop=(w is WL and k == CT - 1))
                last.then_inc(w_used, 1)
            pe.wait_ge(rope_evac, H // G)
            pe.wait_ge(ck_ready, CT)
            pe.wait_ge(kpe_ready, 1)

            with pe.Fori(0, H // G) as g:
                n = Chunk(W_GRP, 6, g)
                def key_tiles(nn, c):
                    pe.wait_ge(w_hi_ready, nn.at(1))
                    for w in (WH, WL):
                        if w is WL:
                            pe.wait_ge(w_lo_ready, nn.at(1))
                        for jj in range(2):
                            for k in range(CT):
                                for x in (CKH, CKL) if w is WH else (CKH,):
                                    last = pe.matmul(PS[:, 2 * c + jj, :], w[:, nn.slot, k * 256 + jj * P:k * 256 + (jj + 1) * P],
                                                     x[:, k * TP:(k + 1) * TP], start=(w is WH and k == 0 and x is CKH),
                                                     stop=(w is WL and k == CT - 1))
                    last.then_inc(w_used, 1)

                def value_tiles(nn, c):
                    pe.wait_ge(w_hi_ready, nn.at(1))
                    for w in (WH, WL):
                        if w is WL:
                            pe.wait_ge(w_lo_ready, nn.at(1))
                        for kk in range(2):
                            k = 2 * c + kk
                            for t in range(QT):
                                for x in (CKH, CKL) if w is WH else (CKH,):
                                    last = pe.matmul(PS[:, 4 + t, :], x[:, k * TP + t * P:k * TP + (t + 1) * P],
                                                     w[:, nn.slot, kk * 512:(kk + 1) * 512],
                                                     start=(w is WH and k == 0 and x is CKH),
                                                     stop=(w is WL and k == CT - 1))
                    last.then_inc(w_used, 1)

                def query_tiles(nn, c):
                    pe.wait_ge(w_hi_ready, nn.at(1))
                    for w in (WH, WL):
                        if w is WL:
                            pe.wait_ge(w_lo_ready, nn.at(1))
                        for jj in range(2):
                            for k in range(CT):
                                for a in range(2):
                                    for x in (QNH, QNL) if w is WH else (QNH,):
                                        last = pe.matmul(PS[:, 4 * c + 2 * jj + a, 0:HALF],
                                                         w[:, nn.slot, k * 256 + jj * P:k * 256 + (jj + 1) * P],
                                                         x[:, k * T + a * HALF:k * T + (a + 1) * HALF],
                                                         start=(w is WH and k == 0 and x is QNH),
                                                         stop=(w is WL and k == CT - 1))
                    last.then_inc(w_used, 1)

                def sample_queries(j):
                    pe.wait_ge(exp_done, g * 16 + (4 * (G - 1) + j + 1))
                    pe.wait_ge(wk_landed[j % 2], (g * 2 + (j // 2 + 1)) * 16)
                    for k in range(CT):
                        last = pe.matmul(PS[:, j, k * P:(k + 1) * P], WK[:, j % 2, k * P:(k + 1) * P],
                                         QN[:, j, T - P:T], start=True, stop=True)
                    last.then_inc(qlat_done, 1)

                def scores(j):
                    r = ROPE * (j % 2)
                    for i in range(QT):
                        if j == 0:
                            pe.wait_ge(k_evac, g * G + (i + 1))
                        else:
                            pe.wait_ge(exp_done, g * 16 + (4 * (j - 1) + i + 1))
                        nk = (i + 1) * P
                        pe.matmul(PS[:, i, 0:nk], QN[:, j, i * P:(i + 1) * P], KTT[:, j * TP:j * TP + nk],
                                  start=True, stop=False)
                        q0 = (j // 2) * TP + i * P
                        pe.matmul(PS[:, i, 0:nk], QPE[r:r + ROPE, q0:q0 + P], KPE[r:r + ROPE, 0:nk],
                                  start=False, stop=True).then_inc(score_done, 1)

                def turn_probs(j):
                    pe.wait_ge(p_ready, g * G + (j + 1))
                    if j == 0:
                        pe.wait_ge(v_evac, g * G + G)
                    else:
                        pe.wait_ge(ptv_evac, g * 8 + 2 * j)
                        pe.wait_ge(pta_evac, g * G + j)
                    s = 0
                    for k in range(QT):
                        for i in range(k, QT):
                            o = P * (i * (i + 1) // 2 + k)
                            last = pe.transpose(PS[:, 4 + s // 4, (s % 4) * P:(s % 4 + 1) * P], PR[:, o:o + P], ident)
                            s += 1
                            if s in (4, 8, 10):
                                last.then_inc(tr_done, 1)

                def values(j):
                    pe.wait_ge(ptv_evac, g * 8 + 2 * (j + 1))
                    pe.wait_ge(pta_evac, g * G + (j + 1))
                    pe.wait_ge(o_done, g * G + j)
                    s = 0
                    for k in range(QT):
                        w = QT - k
                        last = pe.matmul(PS[:, 7, k * P:TP], V[:, k, j * VD:(j + 1) * VD], PT[:, s * P:(s + w) * P],
                                         start=(k == 0), stop=(k == QT - 1))
                        s += w
                    last.then_inc(pv_done, 1)

                pe.wait_ge(qlat_evac, g * G)
                query_tiles(n, 0)
                pe.wait_ge(o_done, g * G)
                query_tiles(n + 1, 1)
                pe.wait_ge(q_evac, g * G + 2)
                key_tiles(n + 2, 0)
                key_tiles(n + 3, 1)
                pe.wait_ge(qpe_ready, g + 1)
                scores(0)
                pe.wait_ge(q_evac, g * G + 4)
                value_tiles(n + 4, 0)
                value_tiles(n + 5, 1)
                for j in range(1, G):
                    scores(j)
                    turn_probs(j - 1)
                    values(j - 1)
                for j in range(G):
                    sample_queries(j)
                turn_probs(G - 1)
                values(G - 1)

            def sample_scores(b, first):
                pe.wait_ge(sq_ready, b + 1)
                pe.wait_ge(pgt_landed, b * (16 * NPG) + 16 * NPG)
                for c in range(3):
                    for k in range(CT):
                        pe.matmul(PS[:, c, 0:3 * P].rearrange("p (a n) -> p a n", a=3), QS[:, k * P:(k + 1) * P],
                                  PG[:, 3 * c:3 * c + 3, k * P:(k + 1) * P], start=(k == 0), stop=False)
                    last = pe.matmul(PS[:, c, 0:3 * P].rearrange("p (a n) -> p a n", a=3), QS[0:ROPE, CT * P:],
                                     PG[0:ROPE, 3 * c:3 * c + 3, CT * P:], start=False, stop=True)
                last.then_inc(sqk_done, 1)
                if not first:
                    pe.wait_ge(olt_evac, b - 1)
                for k in range(CT):
                    last = pe.transpose(PS[0:NS, 3, k * P:(k + 1) * P], PG[:, NPG, k * P:k * P + NS], ident)
                last.then_inc(new_done, 1)

            def sample_turn(b):
                pe.wait_ge(s_exp, b + 1)
                for j in range(NPG):
                    last = pe.transpose(PS[:, 4 + j // 4, (j % 4) * P:(j % 4 + 1) * P], PRS[:, j * P:(j + 1) * P], ident)
                    if j == 3:
                        last.then_inc(str_done, 1)
                last.then_inc(str_done, 1)
                pe.transpose(PS[0:NS, 6, 0:P], PRS[:, PAST:PAST + NS], ident).then_inc(str_done, 1)

            def sample_values(b):
                pe.wait_ge(spt_v, b * 2 + 2)
                pe.wait_ge(spt_a, b + 1)
                pe.wait_ge(new_evac, b + 1)
                pe.wait_ge(nat_landed, b * (16 * NPG) + 16 * NPG)
                for j in range(NPG):
                    pe.matmul(PS[:, 7, :], PTS[:, j * P:(j + 1) * P], NAT[:, j, :], start=(j == 0), stop=False)
                pe.matmul(PS[:, 7, :], PTN[:, :], CKN[:, :], start=False, stop=True).then_inc(spv_done, 1)

            def sample_out_turn(b, new):
                pe.wait_ge(ols_ready, b + 1)
                pe.wait_ge(new_evac, new)
                for k in range(CT):
                    last = pe.transpose(PS[:, 3, k * P:(k + 1) * P], OLS[:, k * P:(k + 1) * P], ident)
                last.then_inc(olt_done, 1)

            pe.wait_ge(qlat_evac, H)
            pe.wait_ge(o_done, H)
            sample_scores(0, True)
            sample_turn(0)
            with pe.Fori(1, NB) as b:
                pe.wait_ge(s_exp, b)
                sample_scores(b, False)
                sample_values(b - 1)
                sample_out_turn(b - 1, b + 1)
                sample_turn(b)
            sample_values(NB - 1)
            sample_out_turn(NB - 1, NB)

            pe.wait_ge(olt_evac, NB)
            with pe.Fori(0, H // 2) as i:
                for s in range(2):
                    pe.wait_ge(wv_landed[s], i * 16 + 16)
                    pe.wait_ge(so_evac, i * 2)
                    for k in range(CT):
                        last = pe.matmul(PS[:, 4 + s, 0:P].rearrange("p (b t) -> p b t", b=NB), WV[:, s, k * VD:(k + 1) * VD],
                                         QLAT[:, k, :, bass.ds(i * (2 * NS), 2 * NS)],
                                         start=(k == 0), stop=(k == CT - 1))
                    last.then_inc(so_done, 1)

            project_out(W_OUT, o_ready, wo)

        @block.scalar
        def _(act):
            def round_w(n):
                if n.i is not None or n.c >= 2:
                    act.wait_ge(w_used, n.at(-1))
                act.wait_ge(raw_landed[n.slot], n.turns() * 16)
                act.activation(WH[:, n.slot, :], WR[:, n.slot, :], ACT.Copy).then_inc(w_hi_ready, 1)

            def root(k, rows=T):
                act.wait_ge(var_ready, k)
                r = RS[(k - 1) % 2]
                act.activation(r[:, :], r[:, :], ACT.Sqrt).then_inc(root_ready, 1)

            act.wait_ge(small_landed, 16)
            act.activation(small("c"), small("c"), ACT.Silu).then_inc(silu_c, 1)
            for k in range(KT):
                if k % 4 == 0:
                    act.wait_ge(x_landed[k // 4], 16)
                if k >= 2:
                    act.wait_ge(xsq_used[k % 2], k // 2)
                act.activation(TT[k % 2][:, :], X[:, k * T:(k + 1) * T], ACT.Square).then_inc(xsq_ready[k % 2], 1)
            root(1)
            round_w(Chunk(0))
            round_w(Chunk(1))

            def round_tiles(raw, hi_done, free=None):
                if free is not None:
                    act.wait_ge(w_used, free)
                for k in range(KT):
                    if raw is not None:
                        act.wait_ge(raw, k + 1)
                    act.activation(OH[:, k * T:(k + 1) * T], B1[:, k * T:(k + 1) * T], ACT.Copy).then_inc(hi_done, 1)

            act.wait_ge(ada_used, 4 * ADA0)
            round_tiles(h_raw, h_hi)

            with act.Fori(0, KT) as m:
                n = Chunk(W_CONV + 2, 8, m)
                for k in range(8):
                    round_w(n + k)
                    if k == 1:
                        act.wait_ge(u_done, m)
                        act.activation(halves(T1[:, :]), pair(0), ACT.Copy).then_inc(c_ready, 1)
                    if k == 5:
                        act.wait_ge(gate_done, m)
                        act.activation(halves(T2[:, :]), pair(0), ACT.Silu).then_inc(z_ready, 1)

            act.wait_ge(gate_done, KT)
            round_tiles(None, y_hi, W_COUT)

            def project_out(w0, s, ahead):
                def body(i, n, split):
                    for j in range(2):
                        if split(j):
                            round_w(n + 2 * j)
                            round_w(n + (2 * j + 1))
                        else:
                            act.wait_ge(w_used, n.at(2 * j))
                        act.wait_ge(s["sq_used"][j], i)
                        act.activation(halves(TT[j][:, :]), pair(j), ACT.Square).then_inc(s["sq"][j], 1)
                        dst = B1[:, bass.ds(i * (2 * T) + j * T, T)]
                        act.activation(halves(dst), pair(j), ACT.Copy).then_inc(s["evac"][j], 1)
                last = KT // 2 if ahead else KT // 2 - 1
                with act.Fori(0, last) as i:
                    body(i, Chunk(w0 + 2, 4, i), lambda j: True)
                if not ahead:
                    body(KT // 2 - 1, Chunk(w0 + 2 + 4 * (KT // 2 - 1)), lambda j: j == 0)

            project_out(W_COUT, co, True)
            root(2)
            for k in range(KT):
                act.wait_ge(x1_ready, k + 1)
                if k >= 2:
                    act.wait_ge(x1sq_used[k % 2], k // 2)
                act.activation(TT[k % 2][:, :], X[:, k * T:(k + 1) * T], ACT.Square).then_inc(x1sq[k % 2], 1)
                xg = B1[:, k * T:(k + 1) * T]
                act.activation(xg, X[:, k * T:(k + 1) * T], ACT.Copy, scale=small("gin", k, 1)).then_inc(xg_hi, 1)
                act.wait_ge(xg_hi, 2 * k + 1)
                act.activation(OH[:, k * T:(k + 1) * T], xg, ACT.Copy).then_inc(xg_hi, 1)
            round_w(Chunk(W_KV + 2))
            root(3)
            for t in range(CT):
                if t:
                    round_w(Chunk(W_KV + 2 * t + 2))
                round_w(Chunk(W_KV + 2 * t + 3))
                act.wait_ge(kv_evac, t + 1)
                if t >= 2:
                    act.wait_ge(kv_sq_used, t - 1)
                act.activation(TT[t % 2][:, :], CKV[:, t * T:(t + 1) * T], ACT.Square).then_inc(kv_sq, 1)
            round_w(Chunk(W_MLA + 1))
            round_tiles(h1_raw, h1_hi, W_MLA)
            root(4)
            act.wait_ge(x_parked, 16)
            act.wait_ge(h1_raw, KT)
            with act.Fori(0, CT // 2) as i:
                n = Chunk(W_MLA + 2, 4, i)
                for j in range(2):
                    round_w(n + 2 * j)
                    round_w(n + (2 * j + 1))
                    act.wait_ge(qa_sq_used[j], i)
                    act.activation(halves(TT[j][:, :]), pair(j), ACT.Square).then_inc(qa_sq[j], 1)
                    act.activation(halves(QA[:, bass.ds(i * (2 * T) + j * T, T)]), pair(j), ACT.Copy).then_inc(qa_evac[j], 1)

            def gate_tiles(i, n):
                for j in range(2):
                    round_w(n + 2 * j)
                    round_w(n + (2 * j + 1))
                    dst = B1[:, bass.ds(i * (2 * T) + j * T, T)]
                    act.activation(halves(dst), pair(j), ACT.Silu).then_inc(z1_evac[j], 1)

            gate_tiles(0, Chunk(W_MLA + 2 * CT + 2))
            root(5)
            for k in range(CT):
                act.wait_ge(qn_raw, k + 1)
                act.activation(QNH[:, k * T:(k + 1) * T], QA[:, k * T:(k + 1) * T], ACT.Copy).then_inc(qn_hi, 1)
            with act.Fori(1, H // 2) as i:
                gate_tiles(i, Chunk(W_MLA + 2 * CT + 2, 4, i))
            act.wait_ge(ckv_ready, CT)
            for k in range(CT):
                act.activation(CKH[:, k * TP:(k + 1) * TP], CKV[:, k * T:k * T + TP], ACT.Copy).then_inc(ck_hi, 1)
            for g in range(H // G):
                round_w(Chunk(W_ROPE + 2 + g))

            with act.Fori(0, H // G) as g:
                n = Chunk(W_GRP + 2, 6, g)
                act.wait_ge(pv_done, g * G)
                act.wait_ge(qn_ready, CT)
                act.wait_ge(qr_ready, H // G)
                act.activation(QPE[:, :], QPA[:, bass.ds(g * (2 * TP), 2 * TP)], ACT.Copy).then_inc(qpe_ready, 1)
                for c in range(2):
                    round_w(n + c)
                    for jj in range(2):
                        act.activation(halves(QN[:, 2 * c + jj, :]), pair(2 * c + jj), ACT.Copy).then_inc(q_evac, 1)
                for c in range(2):
                    round_w(n + (2 + c))
                    for jj in range(2):
                        j = 2 * c + jj
                        act.activation(KTT[:, j * TP:(j + 1) * TP], PS[:, j, :], ACT.Copy).then_inc(k_evac, 1)

                def exps(j):
                    if j:
                        act.wait_ge(tr_done, g * 12 + 3 * j)
                    for i in range(QT):
                        o, w = P * (i * (i + 1) // 2), (i + 1) * P
                        act.wait_ge(bias_ready, g * 16 + (4 * j + i + 1))
                        act.activation(PR[:, o:o + w], PS[:, i, 0:w], ACT.Exp, bias=MX[:, 4 + i:5 + i],
                                       scale=SCALE, accum_out=MX[:, 8 + i:9 + i]).then_inc(exp_done, 1)

                def evac(j):
                    act.wait_ge(tr_done, g * 12 + (3 * j + 2))
                    act.activation(PT[:, 4 * P:8 * P], PS[:, 5, :], ACT.Copy).then_inc(pta_evac, 1)

                exps(0)
                for c in range(2):
                    round_w(n + (4 + c))
                for t in range(QT):
                    act.activation(V[:, t, :], PS[:, 4 + t, :], ACT.Copy).then_inc(v_evac, 1)
                for j in range(1, G):
                    evac(j - 1)
                    exps(j)
                evac(G - 1)

            def sample_exps(b, first):
                act.wait_ge(s_bias, b + 1)
                if not first:
                    act.wait_ge(str_done, b * 3)
                act.activation(PRS[:, 0:6 * P].rearrange("p (a n) -> p a n", a=2), PS[:, 0:2, 0:3 * P], ACT.Exp,
                               bias=MX[:, 4:5], scale=SCALE, accum_out=MX[:, 8:9])
                act.activation(PRS[:, 6 * P:PAST], PS[:, 2, 0:2 * P], ACT.Exp, bias=MX[:, 4:5], scale=SCALE,
                               accum_out=MX[:, 9:10])
                act.activation(PRS[:, PAST:PAST + NS], MX[:, 16:24], ACT.Exp, bias=MX[:, 4:5], scale=SCALE,
                               accum_out=MX[:, 10:11]).then_inc(s_exp, 1)

            def sample_probs(b):
                act.wait_ge(str_done, b * 3 + 2)
                act.activation(PTS[:, 4 * P:8 * P], PS[:, 5, :], ACT.Copy).then_inc(spt_a, 1)

            def sample_out(b):
                act.wait_ge(s_norm, b + 1)
                act.wait_ge(spv_done, b + 1)
                act.activation(OLS[:, :], PS[:, 7, :], ACT.Copy, scale=MX[:, 12:13]).then_inc(ols_ready, 1)

            sample_exps(0, True)
            sample_probs(0)
            with act.Fori(1, NB) as b:
                sample_exps(b, False)
                sample_out(b - 1)
                sample_probs(b)
            sample_out(NB - 1)

            act.wait_ge(so_evac, H)
            round_tiles(None, o_hi)
            project_out(W_OUT, wo, False)
            root(6)

        @block.vector
        def _(dve):
            steps = [0, None]

            def step(ins):
                ins.then_inc(dve_step, 1)
                steps[0] += 1
                if steps[1] is None:
                    dve.wait_ge(dve_step, steps[0])
                else:
                    i, per, first = steps[1]
                    dve.wait_ge(dve_step, (i - first) * per + steps[0] if first else i * per + steps[0])

            def copy(out, in_):
                return dve.tensor_scalar(out, in_, 1.0, None, ALU.mult)

            def loop(first, end, per, body):
                before = steps[0]
                with dve.Fori(first, end) as i:
                    steps[1] = (i, per, first)
                    body(i)
                    assert steps[0] == before + per, (steps[0] - before, per)
                    steps[1] = None
                steps[0] = before + per * (end - first)

            def rstd(k, n):
                r = RS[(k - 1) % 2]
                dve.wait_ge(stat_done, k)
                dve.tensor_scalar(halves(r[:, :]), PS[:, 6:8, 0:HALF], 1.0 / n, EPS, ALU.mult, ALU.add).then_inc(var_ready, 1)
                dve.wait_ge(root_ready, k)
                step(dve.reciprocal(r[:, :], r[:, :]))

            def mod_part(n, bank, before):
                dve.wait_ge(ada_used, n * 4)
                dve.wait_ge(ada_sel, before)
                dve.tensor_copy(PART[:, :], PS[:, bank, 0:AB]).then_inc(ada_part, 1)

            def mod_bias(n, bank, blk):
                dve.wait_ge(ada_sel, n)
                o = _C["bada"][0]
                dve.tensor_tensor(MOD[:, bass.ds(blk * 2, 2), :], PS[:, bank, 0:2 * NM].rearrange("p (a n) -> p a n", a=2),
                                  SM[:, bass.ds(blk * 2 + o, 2)].unsqueeze(2).broadcast_to([P, 2, NM]), ALU.add).then_inc(mod_done, 1)

            def scale_table(src, g, one):
                gb = g.unsqueeze(2).broadcast_to([P, KT, NM])
                step(dve.scalar_tensor_tensor(out=AT[:, :, :], in0=MOD[:, src:src + KT, :], scalar=one, in1=gb,
                                              op0=ALU.add, op1=ALU.mult))

            def modulate(k, shift, raw):
                t = B1[:, k * T:k * T + TP]
                dve.tensor_scalar(t, t, AT[:, k, 0:1], MOD[:, shift + k, 0:1], ALU.mult, ALU.add)
                s = toks(B1[:, k * T + TP:(k + 1) * T])
                step(dve.tensor_tensor(s, s, AT[:, k, 1:NM].unsqueeze(2).broadcast_to([P, NB, NS]), ALU.mult))
                dve.tensor_tensor(s, s, MOD[:, shift + k, 1:NM].unsqueeze(2).broadcast_to([P, NB, NS]), ALU.add).then_inc(raw, 1)

            def rest(k, hi_done, n, ready):
                dve.wait_ge(hi_done, n)
                c = slice(k * T, (k + 1) * T)
                dve.tensor_tensor(OL[:, c], B1[:, c], OH[:, c].bitcast(F32), ALU.subtract).then_inc(ready, 1)

            rstd(1, D)
            dve.wait_ge(small_landed, 16)

            def first_mod(i):
                for q in range(2):
                    mod_part(i * 2 + (q + 1), 4 + q, i * 2 + q)
                    mod_bias(i * 2 + (q + 1), 2 + q, i * 2 + q)
                c = bass.ds(i * (2 * T), 2 * T)
                dve.tensor_tensor(B1[:, c].rearrange("p (a n) -> p a n", a=2), X[:, c].rearrange("p (a n) -> p a n", a=2),
                                  R0[:, :].unsqueeze(1).broadcast_to([P, 2, T]), ALU.mult)

            for q in range(4):
                dve.wait_ge(x_landed[q], 16)
            loop(0, ADA0 // 2, 0, first_mod)
            dve.wait_ge(mod_done, ADA0)
            scale_table(KT, small("gpre", 0, KT), 1.0)
            for k in range(KT):
                modulate(k, 0, h_raw)
                if k:
                    rest(k - 1, h_hi, k, h_ready)
            rest(KT - 1, h_hi, KT, h_ready)

            step(dve.memset(UP[:, 0:2], 0.0))

            def conv(m):
                a = m * 2 + ADA0
                mod_part(m * 2 + (ADA0 + 1), 4, a)
                dve.wait_ge(w_used, m * 8 + 4)
                dve.wait_ge(c_ready, m + 1)
                so = _C["state"][0]
                copy(US[:, :, 0:2], SM[:, bass.ds(m * (2 * NB) + so, 2 * NB)].rearrange("p (b t) -> p b t", b=NB))
                dve.tensor_tensor(UP[:, 2:2 + HALF], PS[:, 2, 0:HALF], T1[:, 0:HALF], ALU.mult)
                dve.tensor_tensor(UP[:, 2 + HALF:2 + TP], PS[:, 3, 0:TP - HALF], T1[:, HALF:TP], ALU.mult)
                dve.tensor_tensor(US[:, :, 2:2 + NS], toks(PS[:, 3, TP - HALF:HALF]), toks(T1[:, TP:T]), ALU.mult).then_inc(u_done, 1)
                dve.wait_ge(u_done, m + 1)
                copy(CST[:, bass.ds(m * 18, 2)], UP[:, TP:TP + 2])
                copy(CST[:, bass.ds(m * 18 + 2, 16)].rearrange("p (b t) -> p b t", b=NB), US[:, :, NS:NS + 2])
                cs = toks(ACC[:, TP:T])
                for k in range(3):
                    w = SM[:, bass.ds(m * 3 + (_C["cw"][0] + k), 1)]
                    if k == 0:
                        dve.tensor_scalar(ACC[:, 0:TP], UP[:, 0:TP], w, None, ALU.mult)
                        step(dve.tensor_scalar(cs, US[:, :, 0:NS], w, None, ALU.mult))
                    else:
                        dve.scalar_tensor_tensor(out=ACC[:, 0:TP], in0=UP[:, k:k + TP], scalar=w, in1=ACC[:, 0:TP],
                                                 op0=ALU.mult, op1=ALU.add)
                        step(dve.scalar_tensor_tensor(out=cs, in0=US[:, :, k:k + NS], scalar=w, in1=cs,
                                                      op0=ALU.mult, op1=ALU.add))
                mod_bias(m * 2 + (ADA0 + 1), 5, a)
                mod_part(m * 2 + (ADA0 + 2), 4, m * 2 + (ADA0 + 1))
                dve.wait_ge(w_used, m * 8 + 8)
                step(dve.tensor_tensor(halves(ACC[:, :]), pair(1), halves(ACC[:, :]), ALU.mult))
                dve.wait_ge(z_ready, m + 1)
                dve.tensor_tensor(B1[:, bass.ds(m * T, T)], ACC[:, :], T2[:, :], ALU.mult).then_inc(gate_done, 1)
                mod_bias(m * 2 + (ADA0 + 2), 5, m * 2 + (ADA0 + 1))

            loop(0, KT, 4, conv)
            dve.wait_ge(gate_done, KT)

            def project_out(hi_done, ready, s):
                for t in range(KT):
                    rest(t, hi_done, t + 1, ready)
                step(dve.memset(ACC[:, :], 0.0))

                def squares(i):
                    for j in range(2):
                        dve.wait_ge(s["sq"][j], i + 1)
                        dve.tensor_tensor(ACC[:, :], ACC[:, :], TT[j][:, :], ALU.add).then_inc(s["sq_used"][j], 1)
                        dve.wait_ge(s["sq_used"][j], i + 1)
                loop(0, KT // 2, 0, squares)

            project_out(y_hi, y_ready, co)

            def residual(k, layer, ready, end):
                rstd(k, D)
                scale_table(48 * layer + 2 * KT, small("gpost", KT * layer, KT), 0.0)
                for j in range(2):
                    dve.wait_ge((co if layer == 0 else wo)["evac"][j], KT // 2)
                r = RS[(k - 1) % 2]
                for t in range(KT):
                    b = B1[:, t * T:(t + 1) * T]
                    step(dve.tensor_tensor(b, b, r[:, :], ALU.mult))
                    xs, bs = toks(X[:, t * T + TP:(t + 1) * T]), toks(B1[:, t * T + TP:(t + 1) * T])
                    dve.scalar_tensor_tensor(out=X[:, t * T:t * T + TP], in0=B1[:, t * T:t * T + TP], scalar=AT[:, t, 0:1],
                                             in1=X[:, t * T:t * T + TP], op0=ALU.mult, op1=ALU.add)
                    step(dve.tensor_tensor(bs, bs, AT[:, t, 1:NM].unsqueeze(2).broadcast_to([P, NB, NS]), ALU.mult))
                    dve.tensor_tensor(xs, xs, bs, ALU.add).then_inc(ready, 1)
                    if end:
                        end(t)

            def rest_xg(t):
                if t:
                    rest(t - 1, xg_hi, 2 * t, xg_ready)

            residual(2, 0, x1_ready, rest_xg)
            rest(KT - 1, xg_hi, 2 * KT, xg_ready)
            step(dve.memset(ACC[:, :], 0.0))
            rstd(3, D)
            scale_table(48 + KT, small("gpre", KT, KT), 1.0)
            for t in range(CT):
                dve.wait_ge(w_used, W_KV + 2 * t + 2)
                dve.tensor_tensor(halves(CKV[:, t * T:(t + 1) * T]), pair(t % 2), halves(R0[:, :]), ALU.mult).then_inc(kv_evac, 1)
                for k in range(4 * t, 4 * t + 4):
                    c = slice(k * T, (k + 1) * T)
                    step(dve.tensor_tensor(B1[:, c], X[:, c], R0[:, :], ALU.mult))
                    modulate(k, 48, h1_raw)
                dve.wait_ge(kv_sq, t + 1)
                dve.tensor_tensor(ACC[:, :], ACC[:, :], TT[t % 2][:, :], ALU.add).then_inc(kv_sq_used, 1)
                dve.wait_ge(kv_sq_used, t + 1)
            dve.wait_ge(w_used, W_MLA)
            dve.wait_ge(rope_landed, 32)
            dve.tensor_tensor(halves(KPE[0:ROPE, :]), pair(0, ROPE), halves(R0[0:ROPE, :]), ALU.mult).then_inc(kv_evac, 1)
            dve.wait_ge(kv_evac, CT + 1)
            for k in range(KT):
                rest(k, h1_hi, k + 1, h1_ready)
            rstd(4, R)
            for t in range(CT):
                c = CKV[:, t * T:(t + 1) * T]
                dve.scalar_tensor_tensor(out=c, in0=c, scalar=small("glat", t, 1), in1=R1[:, :],
                                         op0=ALU.mult, op1=ALU.mult).then_inc(ckv_ready, 1)
            step(dve.tensor_tensor(ACC[0:RH, :], KPE[RH:ROPE, :], SIN[RH:ROPE, :], ALU.mult))
            step(dve.tensor_tensor(ACC[RH:ROPE, :], KPE[0:RH, :], SIN[0:RH, :], ALU.mult))
            step(dve.tensor_tensor(KPE[0:ROPE, :], KPE[0:ROPE, :], COS[0:ROPE, :], ALU.mult))
            step(dve.tensor_tensor(KPE[0:RH, :], KPE[0:RH, :], ACC[0:RH, :], ALU.subtract))
            step(dve.tensor_tensor(KPE[RH:ROPE, :], KPE[RH:ROPE, :], ACC[RH:ROPE, :], ALU.add))
            dve.tensor_copy(KPE[ROPE:P, 0:TP], KPE[0:ROPE, 0:TP]).then_inc(kpe_ready, 1)
            step(dve.memset(ACC[:, :], 0.0))

            def qa_squares(i):
                for j in range(2):
                    dve.wait_ge(qa_sq[j], i + 1)
                    dve.tensor_tensor(ACC[:, :], ACC[:, :], TT[j][:, :], ALU.add).then_inc(qa_sq_used[j], 1)
                    dve.wait_ge(qa_sq_used[j], i + 1)

            loop(0, CT // 2, 0, qa_squares)
            rstd(5, R)
            for j in range(2):
                dve.wait_ge(qa_evac[j], CT // 2)
            for k in range(CT):
                c = QA[:, k * T:(k + 1) * T]
                dve.scalar_tensor_tensor(out=c, in0=c, scalar=small("gq", k, 1), in1=R0[:, :],
                                         op0=ALU.mult, op1=ALU.mult).then_inc(qn_raw, 1)
            for k in range(CT):
                c = slice(k * T, (k + 1) * T)
                dve.wait_ge(qn_hi, k + 1)
                dve.tensor_tensor(QNL[:, c], QA[:, c], QNH[:, c].bitcast(F32), ALU.subtract).then_inc(qn_ready, 1)
            for k in range(CT):
                dve.wait_ge(ck_hi, k + 1)
                dve.tensor_tensor(CKL[:, k * TP:(k + 1) * TP], CKV[:, k * T:k * T + TP],
                                  CKH[:, k * TP:(k + 1) * TP].bitcast(F32), ALU.subtract).then_inc(ck_ready, 1)
            for g in range(H // G):
                dve.wait_ge(w_used, W_ROPE + g + 1)
                for dst, p, tab in ((T1, 0, COS), (T2, 1, SIN), (ACC, 1, COS)):
                    dve.tensor_tensor(halves(dst[:, :]), pair(p), halves(tab[:, :]), ALU.mult)
                dve.tensor_tensor(halves(R1[:, :]), pair(0), halves(SIN[:, :]), ALU.mult).then_inc(rope_evac, 1)
                dve.wait_ge(rope_evac, g + 1)
                for j in range(G):
                    s = slice(RH * j, RH * j + RH)
                    r, c = ROPE * (j % 2), (2 * g + j // 2) * TP
                    dve.tensor_tensor(QPA[r:r + RH, c:c + TP], T1[s, 0:TP], T2[s, 0:TP], ALU.subtract)
                    dve.tensor_tensor(QPA[r + RH:r + ROPE, c:c + TP], ACC[s, 0:TP], R1[s, 0:TP], ALU.add)
                    dve.tensor_tensor(QPS[0:RH, :, G * g + j, :], toks(T1[s, TP:T]), toks(T2[s, TP:T]), ALU.subtract)
                    last = dve.tensor_tensor(QPS[RH:ROPE, :, G * g + j, :], toks(ACC[s, TP:T]), toks(R1[s, TP:T]), ALU.add)
                last.then_inc(qr_ready, 1)
                dve.wait_ge(qr_ready, g + 1)

            def group(g):
                def maxima(j):
                    for i in range(QT):
                        dve.wait_ge(score_done, g * 16 + (4 * j + i + 1))
                        if j:
                            dve.wait_ge(exp_done, g * 16 + (4 * (j - 1) + i + 1))
                        d = PS[:, i, i * P:(i + 1) * P]
                        step(dve.tensor_tensor(d, d, small("mask"), ALU.add))
                        step(dve.tensor_reduce(MX[:, i:i + 1], PS[:, i, 0:(i + 1) * P], AX.X, ALU.max))
                        dve.tensor_scalar(MX[:, 4 + i:5 + i], MX[:, i:i + 1], -SCALE, None, ALU.mult).then_inc(bias_ready, 1)

                def normalise(j):
                    for i in range(QT):
                        o, w = P * (i * (i + 1) // 2), (i + 1) * P
                        dve.wait_ge(exp_done, g * 16 + (4 * j + i + 1))
                        step(dve.reciprocal(MX[:, 12 + i:13 + i], MX[:, 8 + i:9 + i]))
                        last = dve.tensor_scalar(PR[:, o:o + w], PR[:, o:o + w], MX[:, 12 + i:13 + i], None, ALU.mult)
                    last.then_inc(p_ready, 1)

                def out(j):
                    dve.wait_ge(tr_done, g * 12 + (3 * j + 1))
                    dve.tensor_copy(PT[:, 0:4 * P], PS[:, 4, :]).then_inc(ptv_evac, 1)
                    dve.wait_ge(tr_done, g * 12 + (3 * j + 3))
                    dve.tensor_copy(PT[:, 8 * P:10 * P], PS[:, 6, 0:2 * P]).then_inc(ptv_evac, 1)
                    dve.wait_ge(pv_done, g * G + (j + 1))
                    o = B1[:, bass.ds(g * (G * T) + j * T, TP)]
                    dve.tensor_tensor(o, PS[:, 7, :], o, ALU.mult).then_inc(o_done, 1)

                maxima(0)
                normalise(0)
                for j in range(1, G):
                    maxima(j)
                    out(j - 1)
                    normalise(j)
                for j in range(G):
                    dve.wait_ge(qlat_done, g * G + (j + 1))
                    dst = QLAT[:, :, :, bass.ds(g * (G * NS) + j * NS, NS)]
                    src = PS[:, j, :].rearrange("p (k n) -> p k n", k=CT)[:, :, TS:P]
                    copy(dst, src.rearrange("p k (b t) -> p k b t", b=NB)).then_inc(qlat_evac, 1)
                out(G - 1)

            for j in range(2):
                dve.wait_ge(z1_evac[j], H // 2)
            loop(0, H // G, G * QT * 3, group)

            step(dve.memset(PG[:, NPG, :], 0.0))

            def sample_prepare(b, first):
                if not first:
                    dve.wait_ge(new_done, b)
                copy(QS[:, 0:CT * P].rearrange("p (k n) -> p k n", k=CT), QLAT[:, :, bass.ds(b, 1), :].rearrange("p k a n -> p k (a n)"))
                copy(QS[0:ROPE, CT * P:], QPS[:, bass.ds(b, 1), :, :].rearrange("p a h t -> p (a h t)"))
                copy(PG[0:ROPE, NPG, CT * P:CT * P + NS], KPE[0:ROPE, bass.ds(b * NS + TP, NS)])
                copy(PG[:, NPG, 0:CT * P].rearrange("p (k n) -> p k n", k=CT)[:, :, 0:NS],
                     CKV[:, :].rearrange("p (k n) -> p k n", k=CT)[:, :, bass.ds(b * NS + TP, NS)]).then_inc(sq_ready, 1)

            def sample_maxima(b):
                dve.wait_ge(sqk_done, b + 1)
                step(dve.tensor_tensor(MX[:, 16:24], PS[:, 2, 2 * P:2 * P + NS], small("mask8"), ALU.add))
                dve.tensor_reduce(MX[:, 0:1], PS[:, 0:2, 0:3 * P], AX.XY, ALU.max)
                dve.tensor_reduce(MX[:, 1:2], PS[:, 2, 0:2 * P], AX.X, ALU.max)
                step(dve.tensor_reduce(MX[:, 2:3], MX[:, 16:24], AX.X, ALU.max))
                step(dve.tensor_reduce(MX[:, 3:4], MX[:, 0:3], AX.X, ALU.max))
                dve.tensor_scalar(MX[:, 4:5], MX[:, 3:4], -SCALE, None, ALU.mult).then_inc(s_bias, 1)

            def sample_new(b, first):
                dve.wait_ge(new_done, b + 1)
                if not first:
                    dve.wait_ge(spv_done, b)
                dve.tensor_copy(CKN[:, :], PS[0:NS, 3, :]).then_inc(new_evac, 1)

            def sample_probs(b, first):
                dve.wait_ge(s_exp, b + 1)
                step(dve.tensor_reduce(MX[:, 11:12], MX[:, 8:11], AX.X, ALU.add))
                if not first:
                    dve.wait_ge(ols_ready, b)
                dve.reciprocal(MX[:, 12:13], MX[:, 11:12]).then_inc(s_norm, 1)
                dve.wait_ge(str_done, b * 3 + 1)
                dve.tensor_copy(PTS[:, 0:4 * P], PS[:, 4, :]).then_inc(spt_v, 1)
                dve.wait_ge(str_done, b * 3 + 3)
                dve.tensor_copy(PTN[:, :], PS[0:NS, 6, 0:P]).then_inc(spt_v, 1)

            def sample_out(b):
                dve.wait_ge(olt_done, b + 1)
                copy(QLAT[:, :, bass.ds(b, 1), :].rearrange("p k a n -> p k (a n)"),
                     PS[:, 3, :].rearrange("p (k n) -> p k n", k=CT)).then_inc(olt_evac, 1)

            def batch(b):
                sample_prepare(b, False)
                sample_maxima(b)
                sample_new(b, False)
                sample_out(b - 1)
                sample_probs(b, False)

            sample_prepare(0, True)
            sample_maxima(0)
            sample_new(0, True)
            sample_probs(0, True)
            loop(1, NB, 4, batch)
            sample_out(NB - 1)

            def sample_gate(i):
                for s in range(2):
                    dve.wait_ge(so_done, i * 2 + (s + 1))
                    o = B1[:, bass.ds(i * (2 * T) + (s * T + TP), TS)]
                    o = o.rearrange("p (b t) -> p b t", b=NB)
                    mine = PS[:, 4 + s, 0:P].rearrange("p (b t) -> p b t", b=NB)[:, :, s * NS:(s + 1) * NS]
                    dve.tensor_tensor(o, mine, o, ALU.mult).then_inc(so_evac, 1)

            loop(0, H // 2, 0, sample_gate)
            dve.wait_ge(so_evac, H)
            project_out(o_hi, o_ready, wo)
            dve.wait_ge(x1_back, 16)
            residual(6, 1, yout_ready, None)


def kernel(x_prompt, x_sample, state_conv, cache_ckv, cache_kpe, page_table, c_prompt, c_sample,
           w_ada, b_ada, g_pre, g_post, conv_w_in, conv_w, conv_w_out,
           kv_g_in, kv_w_down, kv_g_latent, kv_w_up, mla_w_in, mla_g_q, mla_w_uq, mla_w_out):
    import concourse.bacc as bacc
    from concourse.bass_utils import run_bass_kernel_spmd

    f = lambda a: np.asarray(a)
    (x_prompt, x_sample, state_conv, cache_ckv, cache_kpe, page_table, c_prompt, c_sample, w_ada, b_ada, g_pre,
     g_post, conv_w_in, conv_w, conv_w_out, kv_g_in, kv_w_down, kv_g_latent, kv_w_up, mla_w_in, mla_g_q, mla_w_uq,
     mla_w_out) = map(f, (x_prompt, x_sample, state_conv, cache_ckv, cache_kpe, page_table, c_prompt, c_sample,
                          w_ada, b_ada, g_pre, g_post, conv_w_in, conv_w, conv_w_out, kv_g_in, kv_w_down,
                          kv_g_latent, kv_w_up, mla_w_in, mla_g_q, mla_w_uq, mla_w_out))

    def tiles(a):
        return a.reshape(-1, P, a.shape[-1]).transpose(1, 0, 2).reshape(P, -1)

    def chunks(w, kts, cols):
        k, n = w.shape
        a = w.reshape(k // (kts * P), kts, P, n // cols, cols).transpose(3, 0, 2, 1, 4)
        return a.reshape(-1, P, kts * cols)

    x = np.concatenate([x_prompt[0].T, x_sample.reshape(TS, D).T], axis=1)
    w_in = conv_w_in[0].reshape(D, 4, KT, P)[:, [1, 2, 3, 0]].transpose(0, 2, 1, 3).reshape(D, -1)
    uq = mla_w_uq[0].reshape(R, H, NOPE + ROPE)
    nope = uq[:, :, :NOPE].reshape(R, -1)
    rope = uq[:, :, NOPE:].reshape(R, H // G, G, 2, RH).transpose(0, 1, 3, 2, 4).reshape(R, -1)
    up_k = kv_w_up[:, :, :NOPE].reshape(R, -1)
    up_v = kv_w_up[:, :, NOPE:].reshape(R, -1)
    k_chunks = chunks(up_k, CT, 256).reshape(H // G, 2, P, CH)
    v_chunks = chunks(up_v, 2, 512).reshape(H // G, 2, P, CH)
    q_chunks = chunks(nope, CT, 256).reshape(H // G, 2, P, CH)
    groups = np.concatenate([q_chunks, k_chunks, v_chunks], axis=1).reshape(-1, P, CH)
    wstream = np.concatenate([
        chunks(w_in, 8, P), chunks(conv_w_out[0], 8, P), chunks(kv_w_down[:, :R], 8, P),
        chunks(kv_w_down[:, R:], KT, ROPE), chunks(mla_w_in[0], 8, P), chunks(rope, CT, 256), groups,
        chunks(mla_w_out[0], 8, P)])
    assert wstream.shape[0] == W_END
    ada = np.concatenate([w_ada[0], w_ada[1]], axis=1)
    adastream = ada.reshape(4, 4, P, 48, AB).transpose(3, 0, 2, 1, 4).reshape(48, 4, P, CH)
    c = np.concatenate([c_prompt, c_sample], axis=0)
    cpad = np.concatenate([c.T, np.zeros((D, 32 - NM), np.float32)], axis=1)
    sel = np.zeros((P, NM), np.float32)
    for r in range(NM):
        sel[r::32, r] = 1.0
    q, k = np.arange(P)[:, None], np.arange(P)[None, :]
    mask = np.where(k <= q, 0.0, NEG).astype(np.float32)
    mask8 = np.where(np.arange(NS)[None, :] <= (np.arange(P) % NS)[:, None], 0.0, NEG).astype(np.float32)
    col = lambda a: a.reshape(-1, P).T
    small_in = np.concatenate([
        col(b_ada), col(g_pre), col(g_post), col(kv_g_in), col(kv_g_latent), col(mla_g_q),
        tiles(np.ascontiguousarray(conv_w[0].T)), tiles(cpad),
        tiles(state_conv[0].transpose(2, 0, 1).reshape(D, -1)),
        np.eye(P, dtype=np.float32), np.ones((P, P), np.float32), sel, mask, mask8], axis=1)
    assert small_in.shape == (P, SMALL)
    pos = np.concatenate([np.arange(TP), np.tile(PAST + np.arange(NS), NB)]).astype(np.float32)
    inv = (np.float32(10000.0) ** (-np.arange(RH, dtype=np.float32) / np.float32(RH))).astype(np.float32)
    ang = (pos[None, :] * inv[:, None]).astype(np.float32).astype(np.float64)
    cos_in = np.tile(np.cos(ang).astype(np.float32), (4, 1))
    sin_in = np.tile(np.sin(ang).astype(np.float32), (4, 1))
    ct = cache_ckv.reshape(POOL_PAGES, PAGE, CT, P).transpose(0, 3, 2, 1).reshape(POOL_PAGES, P, -1)
    kp = np.concatenate([cache_kpe.transpose(0, 2, 1), np.zeros((POOL_PAGES, P - ROPE, PAGE), np.float32)], axis=1)
    pages = np.concatenate([ct, kp, cache_ckv], axis=2)
    wk = kv_w_up[:, :, :NOPE].transpose(1, 2, 0)
    wv = kv_w_up[:, :, NOPE:].reshape(CT, P, H, VD).transpose(2, 1, 0, 3).reshape(H, P, -1)

    ins = {"wstream": wstream, "adastream": adastream, "x_in": tiles(x), "small_in": small_in, "cos_in": cos_in,
           "sin_in": sin_in, "pages": pages, "ptab": page_table.reshape(1, -1).astype(np.int32), "wk_in": wk, "wv_in": wv}
    ins = {k: np.ascontiguousarray(v) for k, v in ins.items()}
    nc = bacc.Bacc("TRN2", target_bir_lowering=False, num_devices=1)
    args = {k: nc.dram_tensor(k, v.shape, mybir.dt.from_np(v.dtype), kind="ExternalInput").ap() for k, v in ins.items()}
    outs = {"y_out": (P, KT * T), "cst_out": (P, KT * 18), "ckv_out": (P, CT * T), "kpe_out": (ROPE, T)}
    for k, s in outs.items():
        args[k] = nc.dram_tensor(k, s, F32, kind="ExternalOutput").ap()
    args["x1_park"] = nc.dram_tensor("x1_park", (P, KT * T), F32, kind="Internal").ap()
    build(nc, **args)
    r = run_bass_kernel_spmd(nc, [ins], core_ids=[0]).results[0]

    def rows(a):
        return a.reshape(P, -1, T).transpose(2, 1, 0).reshape(T, -1)

    y, ckv, kpe = rows(r["y_out"]), rows(r["ckv_out"]), r["kpe_out"].T
    cst = r["cst_out"].reshape(P, KT, 18).transpose(2, 1, 0).reshape(18, D)
    c_ = np.ascontiguousarray
    return (c_(y[:TP])[None], c_(y[TP:]).reshape(NB, NS, D), c_(cst[:2])[None, None],
            c_(cst[2:]).reshape(1, NB, 2, D), c_(ckv[:TP])[None], c_(kpe[:TP])[None],
            c_(ckv[TP:]).reshape(NB, NS, R), c_(kpe[TP:]).reshape(NB, NS, ROPE))
```

```python
from contextlib import ExitStack

import numpy as np

import concourse.bass as bass
from concourse import mybir

F32 = mybir.dt.float32
F32R = mybir.dt.float32r
I32 = mybir.dt.int32
ALU = mybir.AluOpType
ACT = mybir.ActivationFunctionType
AX = mybir.AxisListType

P = 128
D = 2048
KT = D // P
TP = 512
NB, NS = 8, 8
TS = NB * NS
T = TP + TS
HALF = T // 2
H = 16
R = 512
CT = R // P
NOPE, ROPE, VD = 128, 64, 128
RH = ROPE // 2
PAST, PAGE = 1024, 128
NPG = PAST // PAGE
POOL_PAGES = 80
BEGUN = 1
SCALE = (NOPE + ROPE) ** -0.5
EPS = 1e-6
NEG = -1e30
G = 4
QT = TP // P
SO_BEGUN = G
CH = 1024
CH3 = 2 * 3 * P
NM = NB + 1
AB = 256
ADA0 = 2 * D // AB
AHEAD = 4
ON_POOL = range(2, KT, 3)

W_THREE = KT // 2
W_CONV = W_THREE + 2
W_COUT = W_CONV + 8 * (KT - 1)
W_KV = W_COUT + KT * 2
W_MLA = W_KV + W_THREE + 2 + 1
W_ROPE = W_MLA + 2 * (CT + H)
W_GRP = W_ROPE + H // G
W_OUT = W_GRP + 6 * (H // G)
W_END = W_OUT + KT * 2

PGT = CT * P + PAGE
PGW = PGT + R

_C = {}
_n = 0
for _name, _w in (("bada", 96), ("gpre", 2 * KT), ("gpost", 2 * KT), ("gin", KT), ("glat", CT), ("gq", CT),
                  ("cw", 3 * KT), ("c", KT * 32), ("state", KT * NB * 2), ("ident", P), ("ones", P),
                  ("sel", NM), ("mask", P), ("mask8", 8)):
    _C[_name] = (_n, _w)
    _n += _w
SMALL = _n


class Chunk:

    def __init__(self, c, k=0, i=None):
        self.c, self.k, self.i = c, k, i

    def __add__(self, d):
        return Chunk(self.c + d, self.k, self.i)

    def at(self, d=0):
        return self.c + d if self.i is None else self.i * self.k + (self.c + d)

    @property
    def slot(self):
        return self.c % 2

    def turns(self):
        return self.c // 2 + 1 if self.i is None else self.i * (self.k // 2) + (self.c // 2 + 1)


def build(nc, wstream, adastream, x_in, small_in, cos_in, sin_in, pages, ptab, wk_in, wv_in,
          y_out, cst_out, ckv_out, kpe_out, x1_park):
    with ExitStack() as ctx:
        base = 16512
        arena_floats = 53200
        ctx.enter_context(nc.sbuf_tensor("arena", [P, arena_floats], F32))
        top = [0]

        def at(name, off, shape, dt=F32):
            n = int(np.prod(shape[1:]))
            assert off + n <= arena_floats, (name, off + n)
            return nc.alloc_sbuf_tensor_at(name, shape, dt, offset=base + 4 * off)

        def place(n):
            off = top[0]
            top[0] += (n + 7) // 8 * 8
            assert top[0] <= arena_floats, top[0]
            return off

        def sem(name):
            return ctx.enter_context(nc.semaphore(name))

        xo = place(KT * T)
        X = at("x_residual", xo, [P, KT * T])
        QA = at("q_latent", xo, [P, CT * T])
        PT = at("probs_t", xo, [P, 10 * P])
        QPE = at("q_rope_group", xo + 1280, [P, 2 * TP])
        KTT = at("k_nope_t", xo + 2304, [P, G * TP])
        QNH = at("q_latent_hi", xo + 4608, [P, CT * T], F32R)
        QNL = at("q_latent_lo", xo + 6912, [P, CT * T], F32R)
        OLS = at("sample_out_latent", xo, [P, R])
        CKN = at("new_latent", xo + 512, [NS, R])
        NAT_LAST = at("page_latent_last", xo + 1024, [P, NPG, R])
        bo = place(KT * T)
        B1 = at("tiles", bo, [P, KT * T])
        HX = at("h_ring", bo, [P, 4 * T])
        ADA_FIRST = at("ada_first_ring", bo + KT * T - 4 * CH, [P, 4, CH])
        WR = at("w_raw", place(2 * CH), [P, 2, CH])
        WH = at("w_hi", place(2 * CH), [P, 2, CH], F32R)
        WL = at("w_lo", place(2 * CH), [P, 2, CH], F32R)
        po = place(2 * KT * T)
        OH = at("operand_hi", po, [P, KT * T], F32R)
        OL = at("operand_lo", po + KT * T, [P, KT * T], F32R)
        CKH = at("latent_hi", po, [P, CT * TP], F32R)
        CKL = at("latent_lo", po + 2048, [P, CT * TP], F32R)
        QPA = at("q_rope_all", po + 4096, [P, (H // 2) * TP])
        QN = at("q_nope", po + 8192, [P, G, T])
        V = at("values", po + 10496, [P, QT, G * VD])
        QLAT = at("q_lat", po + 12544, [P, CT, NB, P])
        QPS = at("q_rope_sample", po + 16640, [ROPE, NB, H, NS])
        PG = at("page_t", po, [P, NPG + 1, PGT])
        NAT = at("page_latent", po + 5760, [P, NPG, R])
        PTS = at("probs_t_sample", po + 9856, [P, NPG * P])
        PTN = at("probs_t_new", po + 10880, [NS, P])
        QS = at("q_batch", po + 11008, [P, CT * P + P])
        WV = at("wv_ring", po, [P, G, CT * VD])
        ao = place(4 * CH)
        ADA_RING = at("ada_ring", ao, [P, 4, CH])
        COS = at("cos", ao, [P, T])
        SIN = at("sin", ao + T, [P, T])
        WK = [at("wk0", ao, [P, CT * P]), at("wk1", ao + CT * P, [P, CT * P]), at("wk2", po + 17664, [P, CT * P])]
        CKV = at("latent", ao + 2 * T, [P, CT * T])
        KPE = at("k_rope", ao + 2 * T + CT * T, [P, T])
        MOD = at("mod", place(96 * NM), [P, 96, NM])
        SM = at("small", place(SMALL), [P, SMALL])
        AT = at("mod_scale", place(KT * NM), [P, KT, NM])
        CST = at("conv_state", place(KT * 18), [P, KT * 18])
        PART = at("ada_part", place(AB), [P, AB])
        MX = at("row_stats", place(24), [P, 24])
        PTB = at("page_ids", place(NB * NPG), [1, NB * NPG], I32)
        ro = place(T)
        R0 = at("rstd0", ro, [P, T])
        uo = place(TP + 8 + NB * (NS + 2))
        UP = at("u_prompt", uo, [P, TP + 2])
        US = at("u_sample", uo + TP + 8, [P, NB, NS + 2])
        R1 = at("rstd1", uo, [P, T])
        WK.append(at("wk3", ro, [P, CT * P]))
        to = place(3 * T)
        T1 = at("tmp1", to, [P, T])
        T2 = at("tmp2", to + T, [P, T])
        ACC = at("acc", to + 2 * T, [P, T])
        PR = at("probs", to, [P, 10 * P])
        PRS = at("probs_sample", to, [P, PAST + NS])
        RS = [R0, R1]
        TT = [T1, T2]
        PS = ctx.enter_context(nc.psum_tensor("ps", [P, 8, 512], F32))

        def small(name, lo=0, n=None):
            o, w = _C[name]
            return SM[:, o + lo:o + (w if n is None else lo + n)]

        ident = small("ident")

        def pair(p, rows=P):
            return PS[0:rows, 2 * p:2 * p + 2, 0:HALF]

        def halves(ap):
            return ap.rearrange("p (a n) -> p a n", a=2)

        def toks(ap):
            return ap.rearrange("p (b t) -> p b t", b=NB)

        raw_landed = [sem(f"raw_landed{i}") for i in range(2)]
        w_hi_ready, w_lo_ready, w_used = sem("w_hi_ready"), sem("w_lo_ready"), sem("w_used")
        small_landed, x_landed = sem("small_landed"), [sem(f"x_landed{i}") for i in range(4)]
        rope_landed, ptab_landed = sem("rope_landed"), sem("ptab_landed")
        ada0_landed = [sem(f"ada0_landed{i}") for i in range(4)]
        ada_landed = [sem(f"ada_landed{i}") for i in range(4)]
        ada_used, ada_part, ada_sel, mod_done = sem("ada_used"), sem("ada_part"), sem("ada_sel"), sem("mod_done")
        silu_c, stat_done = sem("silu_c"), sem("stat_done")
        var_ready, root_ready = sem("var_ready"), sem("root_ready")
        xsq_ready, xsq_used = [sem(f"xsq_ready{i}") for i in range(2)], [sem(f"xsq_used{i}") for i in range(2)]
        h_raw, h_hi, h_ready = sem("h_raw"), sem("h_hi"), sem("h_ready")
        c_ready, u_done, z_ready, gate_done = sem("c_ready"), sem("u_done"), sem("z_ready"), sem("gate_done")
        y_hi, y_ready = sem("y_hi"), sem("y_ready")
        co = {k: [sem(f"co_{k}{i}") for i in range(2)] for k in ("sq", "sq_used", "evac", "scaled")}
        x1_ready, x1sq, x1sq_used = sem("x1_ready"), [sem(f"x1sq{i}") for i in range(2)], [sem(f"x1sq_used{i}") for i in range(2)]
        xg_hi, xg_ready, x_parked = sem("xg_hi"), sem("xg_ready"), sem("x_parked")
        kv_evac, kv_sq, kv_sq_used = sem("kv_evac"), sem("kv_sq"), sem("kv_sq_used")
        h1_normed, h1_prompt_done = sem("h1_normed"), sem("h1_prompt_done")
        h1_raw, h1_hi, h1_ready = sem("h1_raw"), sem("h1_hi"), sem("h1_ready")
        ckv_ready, kpe_ready = sem("ckv_ready"), sem("kpe_ready")
        qa_sq, qa_sq_used, qa_evac = ([sem(f"{k}{i}") for i in range(2)] for k in ("qa_sq", "qa_sq_used", "qa_evac"))
        z1_evac = [sem(f"z1_evac{i}") for i in range(2)]
        qn_raw, qn_hi, qn_ready = sem("qn_raw"), sem("qn_hi"), sem("qn_ready")
        rope_evac, qr_ready, ck_hi, ck_ready = sem("rope_evac"), sem("qr_ready"), sem("ck_hi"), sem("ck_ready")
        wk_landed = [sem(f"wk_landed{i}") for i in range(G)]
        k_evac, v_evac, q_evac, qpe_ready = sem("k_evac"), sem("v_evac"), sem("q_evac"), sem("qpe_ready")
        qlat_done, qlat_evac = sem("qlat_done"), sem("qlat_evac")
        score_done, bias_ready, exp_done, p_ready = sem("score_done"), sem("bias_ready"), sem("exp_done"), sem("p_ready")
        tr_done, ptv_evac, pta_evac, pv_done, o_done = (sem(n) for n in ("tr_done", "ptv_evac", "pta_evac", "pv_done", "o_done"))
        pgt_landed, nat_landed, last_landed = sem("pgt_landed"), sem("nat_landed"), sem("last_landed")
        sq_ready, sqk_done, new_done, new_evac = sem("sq_ready"), sem("sqk_done"), sem("new_done"), sem("new_evac")
        s_bias, s_exp, s_norm = sem("s_bias"), sem("s_exp"), sem("s_norm")
        str_done, spt_v, spt_a, spv_done, ols_ready, olt_done, olt_evac = (
            sem(n) for n in ("str_done", "spt_v", "spt_a", "spv_done", "ols_ready", "olt_done", "olt_evac"))
        wv_landed = [sem(f"wv_landed{i}") for i in range(G)]
        so_done, so_evac = sem("so_done"), sem("so_evac")
        o_hi, o_ready = sem("o_hi"), sem("o_ready")
        wo = {k: [sem(f"wo_{k}{i}") for i in range(2)] for k in ("sq", "sq_used", "evac", "scaled")}
        x1_back, out_rstd = sem("x1_back"), sem("out_rstd")
        normed, normed_pool = sem("normed"), sem("normed_pool")
        yout_ready, yout_pool = sem("yout_ready"), sem("yout_pool")
        dve_step = sem("dve_step")
        stored = sem("stored")

        block = ctx.enter_context(nc.Block())

        @block.sync
        def _(sp):
            def load_w(n, width=CH):
                if n.i is not None or n.c >= 2:
                    sp.wait_ge(w_lo_ready, n.at(-1))
                src = wstream[bass.ds(n.at(), 1), :, 0:width].rearrange("a p n -> p (a n)")
                sp.dma_start(WR[:, n.slot, 0:width], src).then_inc(raw_landed[n.slot], 16)

            def load_ada(blk, j, dst, landed):
                src = adastream[bass.ds(blk, 1), bass.ds(j, 1), :, :].rearrange("a b p n -> p (a b n)")
                sp.dma_start(dst, src).then_inc(landed, 16)

            sp.dma_start(SM[:, :], small_in).then_inc(small_landed, 16)
            for q in range(4):
                w = KT * T // 4
                sp.dma_start(X[:, q * w:(q + 1) * w], x_in[:, q * w:(q + 1) * w]).then_inc(x_landed[q], 16)
            sp.dma_start(PTB[:, :], ptab).then_inc(ptab_landed, 16)
            load_w(Chunk(0), CH3)
            load_w(Chunk(1), CH3)
            for i in range(ADA0 // 2):
                for q, (dst, landed) in enumerate(((ADA_FIRST, ada0_landed), (ADA_RING, ada_landed))):
                    for j in range(4):
                        if i:
                            sp.wait_ge(ada_used, i * 8 + (4 * q + j + 1 - 8))
                        load_ada(i + q * (ADA0 // 2), j, dst[:, j, :], landed[j])
                if i:
                    load_w(Chunk(i + 1), CH3 if i + 1 < W_THREE else CH)
            for j in range(4):
                sp.wait_ge(ada_used, 4 * (ADA0 - 1) + j + 1)
                load_ada(ADA0, j, ADA_RING[:, j, :], ada_landed[j])
            load_w(Chunk(W_CONV - 1))
            for k in range(8):
                if k in (2, 5):
                    load_w(Chunk(W_CONV + k // 3))
                q, j = k // 4, k % 4
                sp.wait_ge(ada_used, 4 * ADA0 + 4 * q + j + 1)
                load_ada(ADA0 + 1 + q, j, ADA_RING[:, j, :], ada_landed[j])

            def conv_loads(m, n, last):
                for k in range(8):
                    load_w(n + k)
                    q, j = k // 4, k % 4
                    if q == 0 or not last:
                        sp.wait_ge(ada_used, m * 8 + (4 * ADA0 + 4 * q + j + 1))
                        load_ada(m * 2 + (ADA0 + 1 + q), j, ADA_RING[:, j, :], ada_landed[j])

            with sp.Fori(1, KT - 1) as m:
                conv_loads(m, Chunk(W_CONV - 8 + 2, 8, m), False)
            conv_loads(KT - 1, Chunk(W_COUT - 8 + 2), True)
            sp.wait_ge(ada_used, 4 * 48)
            sp.dma_start(COS[:, :], cos_in).then_inc(rope_landed, 16)
            sp.dma_start(SIN[:, :], sin_in).then_inc(rope_landed, 16)
            sp.wait_ge(gate_done, KT)
            sp.dma_start(cst_out, CST[:, :]).then_inc(stored, 16)
            with sp.Fori(0, (W_KV - W_COUT) // 2) as i:
                for k in range(2):
                    load_w(Chunk(W_COUT + 2 + k, 2, i))
            for n in range(W_KV + 2, W_MLA + 2):
                load_w(Chunk(n))
                if n == W_MLA:
                    sp.wait_ge(x1_ready, KT)
                    sp.dma_start(x1_park, X[:, :]).then_inc(x_parked, 16)
            with sp.Fori(0, (W_ROPE - W_MLA) // 2) as i:
                for k in range(2):
                    load_w(Chunk(W_MLA + 2 + k, 2, i))
            for n in range(W_ROPE + 2, W_GRP + 2):
                load_w(Chunk(n))
            sp.wait_ge(ckv_ready, CT)
            sp.dma_start(ckv_out, CKV[:, :]).then_inc(stored, 16)
            sp.wait_ge(kpe_ready, 1)
            sp.dma_start(kpe_out, KPE[0:ROPE, :]).then_inc(stored, 16)

            def load_wk(h, s):
                sp.dma_start(WK[s][:, :], wk_in[bass.ds(h, 1), :, :].rearrange("a p n -> p (a n)")).then_inc(wk_landed[s], 16)

            sp.wait_ge(rope_evac, H // G)
            for j in range(G):
                load_wk(j, j)

            def load_pages(b, dst, lo, hi, landed, used, per=0):
                for j in range(NPG):
                    pid = sp.value_load(PTB[0:1, bass.ds(b * NPG + j, 1)], min_val=0, max_val=POOL_PAGES - 1)
                    if j % 3 == 0 and used is not None and (j == 0 or per):
                        sp.wait_ge(used[0], used[1] + j // 3 * per)
                    sp.dma_start(dst[:, j, :], pages[bass.ds(pid, 1), :, lo:hi].rearrange("a p n -> p (a n)")).then_inc(landed, 16)

            def load_keys(b, used=None):
                load_pages(b, PG, 0, PGT, pgt_landed, used, 1)

            def load_latents(b, used=None):
                load_pages(b, NAT, PGT, PGW, nat_landed, used)

            def group_loads(g, n, last):
                for k in range(6):
                    load_w(n + k)
                if last:
                    sp.wait_ge(ptab_landed, 16)
                    sp.wait_ge(w_used, W_OUT)
                    sp.wait_ge(qpe_ready, H // G)
                    load_keys(0)
                for j in range(0 if last else G):
                    sp.wait_ge(qlat_done, g * G + (j + 1))
                    load_wk(g * G + (j + G), j)

            with sp.Fori(0, H // G - 1) as g:
                group_loads(g, Chunk(W_GRP + 2, 6, g), False)
            group_loads(H // G - 1, Chunk(W_GRP + 2 + 6 * (H // G - 1)), True)
            sp.wait_ge(qlat_done, H)
            load_latents(0)
            load_keys(1, (sqk_done, 1))
            sp.wait_ge(pv_done, H + BEGUN)
            load_pages(NB - 1, NAT_LAST, PGT, PGW, last_landed, None)
            with sp.Fori(1, NB - 1) as b:
                load_keys(b + 1, (sqk_done, b * 3 + 1))
                load_latents(b, (spv_done, b))

            def load_wv(h, s):
                sp.dma_start(WV[:, s, :], wv_in[bass.ds(h, 1), :, :].rearrange("a p n -> p (a n)")).then_inc(wv_landed[s], 16)

            sp.wait_ge(new_done, NB)
            for s in range(G):
                load_wv(s, s)
            with sp.Fori(1, H // G) as i:
                for s in range(G):
                    sp.wait_ge(so_done, i * G + (s + 1 - G))
                    load_wv(i * G + s, s)
            sp.wait_ge(olt_evac, NB + BEGUN)
            sp.dma_start(X[:, :], x1_park).then_inc(x1_back, 16)
            with sp.Fori(0, (W_END - W_OUT - 2) // 2) as i:
                for k in range(2):
                    load_w(Chunk(W_OUT + 2 + k, 2, i))
            for kt in range(KT):
                pooled = len([t for t in ON_POOL if t <= kt])
                if kt in ON_POOL:
                    sp.wait_ge(yout_pool, pooled)
                else:
                    sp.wait_ge(yout_ready, kt + 1 - pooled)
                sp.dma_start(y_out[:, kt * T:(kt + 1) * T], X[:, kt * T:(kt + 1) * T]).then_inc(stored, 16)
            sp.wait_ge(stored, 16 * (3 + KT))

        @block.gpsimd
        def _(pool):
            def rest(n, width=CH):
                pool.wait_ge(w_hi_ready, n.at(1))
                pool.tensor_tensor(WL[:, n.slot, 0:width], WR[:, n.slot, 0:width], WH[:, n.slot, 0:width].bitcast(F32),
                                   ALU.subtract).then_inc(w_lo_ready, 1)

            with pool.Fori(0, W_THREE // 2) as i:
                rest(Chunk(0, 2, i), CH3)
                rest(Chunk(1, 2, i), CH3)
            with pool.Fori(W_THREE // 2, W_END // 2) as i:
                rest(Chunk(0, 2, i))
                rest(Chunk(1, 2, i))
            rest(Chunk(W_END - 1))

            pool.wait_ge(x1_back, 16)
            pool.wait_ge(wo["scaled"][0], KT // 2)
            pool.wait_ge(wo["scaled"][1], KT // 2)
            pool.wait_ge(out_rstd, 1)
            tiles = list(ON_POOL)

            def add(n):
                c = slice(tiles[n] * T, (tiles[n] + 1) * T)
                pool.wait_ge(normed_pool, n + 1)
                pool.tensor_tensor(X[:, c], X[:, c], B1[:, c], ALU.add).then_inc(yout_pool, 1)

            for n, t in enumerate(tiles):
                c = slice(t * T, (t + 1) * T)
                pool.tensor_tensor(B1[:, c], B1[:, c], R1[:, :], ALU.mult).then_inc(normed_pool, 1)
                if n:
                    add(n - 1)
            add(len(tiles) - 1)

        @block.tensor
        def _(pe):
            def tile(n, p, ready=None, each=None, hi=OH, lo=OL, kts=KT, cols=P, split=2):
                per = kts // split
                last = None
                for q in range(split):
                    c = n + q
                    pe.wait_ge(w_hi_ready, c.at(1))
                    for kk in range(per):
                        k = q * per + kk
                        if each:
                            each(k)
                        if ready:
                            pe.wait_ge(ready, k + 1)
                        for a in range(2):
                            for x in (hi, lo):
                                pe.matmul(PS[0:cols, 2 * p + a, 0:HALF], WH[:, c.slot, kk * cols:(kk + 1) * cols],
                                          x[:, k * T + a * HALF:k * T + (a + 1) * HALF],
                                          start=(k == 0 and x is hi), stop=False)
                    pe.wait_ge(w_lo_ready, c.at(1))
                    for kk in range(per):
                        k = q * per + kk
                        for a in range(2):
                            last = pe.matmul(PS[0:cols, 2 * p + a, 0:HALF], WL[:, c.slot, kk * cols:(kk + 1) * cols],
                                             hi[:, k * T + a * HALF:k * T + (a + 1) * HALF],
                                             start=False, stop=(k == kts - 1))
                    last.then_inc(w_used, 1)

            def three_tiles(n, i, ready, each=None):
                for w in (WH, WL):
                    pe.wait_ge(w_hi_ready if w is WH else w_lo_ready, n.at(1))
                    for kk in range(2):
                        k = 2 * i + kk
                        if w is WH:
                            if each:
                                each(k)
                            pe.wait_ge(ready, k + 1)
                        for t in range(3):
                            for a in range(2):
                                for x in (OH, OL) if w is WH else (OH,):
                                    last = pe.matmul(PS[:, 2 * t + a, 0:HALF], w[:, n.slot, (3 * kk + t) * P:(3 * kk + t + 1) * P],
                                                     x[:, k * T + a * HALF:k * T + (a + 1) * HALF],
                                                     start=(w is WH and k == 0 and x is OH),
                                                     stop=(w is WL and k == KT - 1))
                last.then_inc(w_used, 1)

            def ada_block(ring, landed, turns, bank):
                for j in range(4):
                    pe.wait_ge(landed[j], turns * 16)
                    for g in range(4):
                        k = 4 * j + g
                        last = pe.matmul(PS[32 * g:32 * g + 32, bank, 0:AB], small("c", 32 * k, 32),
                                         ring[:, j, g * AB:(g + 1) * AB],
                                         start=(j == 0), stop=(j == 3), skip_group_check=True)
                    last.then_inc(ada_used, 1)

            def ada_select(n, bank, before):
                pe.wait_ge(ada_part, n)
                if before is not None:
                    pe.wait_ge(mod_done, before)
                for q in range(2):
                    last = pe.matmul(PS[:, bank, q * NM:(q + 1) * NM], PART[:, q * P:(q + 1) * P], small("sel"),
                                     start=True, stop=True)
                last.then_inc(ada_sel, 1)

            def column_sums(added, n):
                for s in added:
                    pe.wait_ge(s, n + BEGUN)
                for a in range(2):
                    last = pe.matmul(PS[:, 6 + a, 0:HALF], small("ones"), ACC[:, a * HALF:(a + 1) * HALF],
                                     start=True, stop=True)
                last.then_inc(stat_done, 1)

            def add_squares(ready, used, k, n):
                pe.wait_ge(ready[k % 2], k // 2 + 1)
                for a in range(2):
                    last = pe.matmul(PS[:, 6 + a, 0:HALF], small("ones"), TT[k % 2][:, a * HALF:(a + 1) * HALF],
                                     start=(k == 0), stop=(k == n - 1), skip_group_check=True)
                last.then_inc(used[k % 2] if k < n - 1 else stat_done, 1)

            pe.sem_inc(pv_done, BEGUN)
            pe.wait_ge(small_landed, 16)
            for k in range(KT):
                add_squares(xsq_ready, xsq_used, k, KT)
            pe.wait_ge(silu_c, 1)
            pe.wait_ge(var_ready, 1)
            for i in range(ADA0 // 2):
                for q in range(2):
                    b = 2 * i + q
                    ada_block(*((ADA_FIRST, ada0_landed), (ADA_RING, ada_landed))[q], i + 1, 6)
                    ada_select(b + 1, 7, b if b else None)
                if i:
                    three_tiles(Chunk(i - 1), i - 1, h_ready)
            three_tiles(Chunk(W_THREE - 1), W_THREE - 1, h_ready)

            ada_block(ADA_RING, ada_landed, ADA0 // 2 + 1, 6)
            ada_select(ADA0 + 1, 7, ADA0)
            pe.wait_ge(u_done, 1)
            tile(Chunk(W_THREE), 1)
            ada_block(ADA_RING, ada_landed, ADA0 // 2 + 2, 6)
            ada_select(ADA0 + 2, 7, ADA0 + 1)
            with pe.Fori(1, KT) as m:
                n = Chunk(W_CONV - 8, 8, m)
                pe.wait_ge(z_ready, m)
                tile(n, 0)
                ada_block(ADA_RING, ada_landed, m * 2 + (ADA0 // 2 + 1), 6)
                pe.wait_ge(gate_done, m)
                tile(n + 2, 1)
                ada_select(m * 2 + (ADA0 + 1), 7, m * 2 + ADA0)
                pe.wait_ge(c_ready, m + 1)
                tile(n + 4, 0)
                ada_block(ADA_RING, ada_landed, m * 2 + (ADA0 // 2 + 2), 6)
                pe.wait_ge(u_done, m + 1)
                tile(n + 6, 1)
                ada_select(m * 2 + (ADA0 + 2), 7, m * 2 + (ADA0 + 1))

            def project_out(w0, ready, s):
                with pe.Fori(0, KT // 2) as i:
                    for j in range(2):
                        pe.wait_ge(s["evac"][j], i + BEGUN)
                        tile(Chunk(w0 + 2 * j, 4, i), j, ready=ready if j == 0 else None)
                column_sums(s["sq_used"], KT // 2)

            pe.wait_ge(z_ready, KT)
            pe.wait_ge(gate_done, KT)
            project_out(W_COUT, y_ready, co)

            pe.wait_ge(var_ready, 2)
            for j in range(2):
                pe.wait_ge(co["evac"][j], KT // 2 + BEGUN)
            for i in range(W_THREE):
                three_tiles(Chunk(W_KV + i), i, xg_ready, each=lambda k: add_squares(x1sq, x1sq_used, k, KT))
            pe.wait_ge(var_ready, 3)
            tile(Chunk(W_KV + W_THREE), 3)
            pe.wait_ge(kv_evac, 3)
            tile(Chunk(W_KV + W_THREE + 2), 2, cols=ROPE, split=1)
            column_sums([kv_sq_used], CT)

            with pe.Fori(0, CT // 2) as i:
                for j in range(2):
                    pe.wait_ge(qa_evac[j], i + BEGUN)
                    tile(Chunk(W_MLA + 2 * j, 4, i), j, ready=h1_ready if j == 0 else None)

            def gate_tiles(i, n):
                for j in range(2):
                    pe.wait_ge(z1_evac[j], i + BEGUN)
                    tile(n + 2 * j, j)

            for j in range(2):
                pe.wait_ge(qa_evac[j], CT // 2 + BEGUN)
            gate_tiles(0, Chunk(W_MLA + 2 * CT))
            column_sums(qa_sq_used, CT // 2)
            with pe.Fori(1, H // 2) as i:
                gate_tiles(i, Chunk(W_MLA + 2 * CT, 4, i))
            for j in range(2):
                pe.wait_ge(z1_evac[j], H // 2 + BEGUN)

            pe.wait_ge(qn_ready, CT)
            for g in range(H // G):
                n = Chunk(W_ROPE + g)
                if g >= 2:
                    pe.wait_ge(rope_evac, g - 1)
                pe.wait_ge(w_hi_ready, n.at(1))
                for w in (WH, WL):
                    if w is WL:
                        pe.wait_ge(w_lo_ready, n.at(1))
                    for k in range(CT):
                        for p in range(2):
                            for a in range(2):
                                for x in (QNH, QNL) if w is WH else (QNH,):
                                    last = pe.matmul(PS[:, 4 * (g % 2) + 2 * p + a, 0:HALF],
                                                     w[:, n.slot, k * 256 + p * P:k * 256 + (p + 1) * P],
                                                     x[:, k * T + a * HALF:k * T + (a + 1) * HALF],
                                                     start=(w is WH and k == 0 and x is QNH),
                                                     stop=(w is WL and k == CT - 1))
                last.then_inc(w_used, 1)
            pe.wait_ge(rope_evac, H // G - 1)
            pe.wait_ge(ck_ready, CT)
            pe.wait_ge(kpe_ready, 1)

            with pe.Fori(0, H // G) as g:
                n = Chunk(W_GRP, 6, g)
                def key_tiles(nn, c):
                    pe.wait_ge(w_hi_ready, nn.at(1))
                    for w in (WH, WL):
                        if w is WL:
                            pe.wait_ge(w_lo_ready, nn.at(1))
                        for jj in range(2):
                            for k in range(CT):
                                for x in (CKH, CKL) if w is WH else (CKH,):
                                    last = pe.matmul(PS[:, 2 * c + jj, :], w[:, nn.slot, k * 256 + jj * P:k * 256 + (jj + 1) * P],
                                                     x[:, k * TP:(k + 1) * TP], start=(w is WH and k == 0 and x is CKH),
                                                     stop=(w is WL and k == CT - 1))
                    last.then_inc(w_used, 1)

                def value_tiles(nn, c):
                    pe.wait_ge(w_hi_ready, nn.at(1))
                    for w in (WH, WL):
                        if w is WL:
                            pe.wait_ge(w_lo_ready, nn.at(1))
                        for kk in range(2):
                            k = 2 * c + kk
                            for t in range(QT):
                                for x in (CKH, CKL) if w is WH else (CKH,):
                                    last = pe.matmul(PS[:, 4 + t, :], x[:, k * TP + t * P:k * TP + (t + 1) * P],
                                                     w[:, nn.slot, kk * 512:(kk + 1) * 512],
                                                     start=(w is WH and k == 0 and x is CKH),
                                                     stop=(w is WL and k == CT - 1))
                    last.then_inc(w_used, 1)

                def query_tiles(nn, c):
                    pe.wait_ge(w_hi_ready, nn.at(1))
                    for w in (WH, WL):
                        if w is WL:
                            pe.wait_ge(w_lo_ready, nn.at(1))
                        for jj in range(2):
                            for k in range(CT):
                                for a in range(2):
                                    for x in (QNH, QNL) if w is WH else (QNH,):
                                        last = pe.matmul(PS[:, 4 * c + 2 * jj + a, 0:HALF],
                                                         w[:, nn.slot, k * 256 + jj * P:k * 256 + (jj + 1) * P],
                                                         x[:, k * T + a * HALF:k * T + (a + 1) * HALF],
                                                         start=(w is WH and k == 0 and x is QNH),
                                                         stop=(w is WL and k == CT - 1))
                    last.then_inc(w_used, 1)

                def sample_queries(j):
                    pe.wait_ge(exp_done, g * 16 + (4 * (G - 1) + j + 1))
                    pe.wait_ge(wk_landed[j], g * 16 + 16)
                    for k in range(CT):
                        last = pe.matmul(PS[:, j, k * P:(k + 1) * P], WK[j][:, k * P:(k + 1) * P],
                                         QN[:, j, T - P:T], start=True, stop=True)
                    last.then_inc(qlat_done, 1)

                def scores(j):
                    r = ROPE * (j % 2)
                    for i in range(QT):
                        if j == 0:
                            pe.wait_ge(k_evac, g * G + (i + 1))
                        else:
                            pe.wait_ge(exp_done, g * 16 + (4 * (j - 1) + i + 1))
                        nk = (i + 1) * P
                        pe.matmul(PS[:, i, 0:nk], QN[:, j, i * P:(i + 1) * P], KTT[:, j * TP:j * TP + nk],
                                  start=True, stop=False)
                        q0 = (j // 2) * TP + i * P
                        pe.matmul(PS[:, i, 0:nk], QPE[r:r + ROPE, q0:q0 + P], KPE[r:r + ROPE, 0:nk],
                                  start=False, stop=True).then_inc(score_done, 1)

                def turn_probs(j):
                    pe.wait_ge(p_ready, g * G + (j + 1))
                    if j == 0:
                        pe.wait_ge(v_evac, g * G + G)
                    else:
                        pe.wait_ge(ptv_evac, g * 8 + 2 * j)
                        pe.wait_ge(pta_evac, g * G + j)
                    s = 0
                    for k in range(QT):
                        for i in range(k, QT):
                            o = P * (i * (i + 1) // 2 + k)
                            last = pe.transpose(PS[:, 4 + s // 4, (s % 4) * P:(s % 4 + 1) * P], PR[:, o:o + P], ident)
                            s += 1
                            if s in (4, 8, 10):
                                last.then_inc(tr_done, 1)

                def values(j):
                    pe.wait_ge(ptv_evac, g * 8 + (2 * j + 1))
                    pe.wait_ge(o_done, g * G + (j + BEGUN))
                    s = 0
                    for k in range(QT):
                        if k == 1:
                            pe.wait_ge(pta_evac, g * G + (j + 1))
                        if k == 2:
                            pe.wait_ge(ptv_evac, g * 8 + (2 * j + 2))
                        w = QT - k
                        last = pe.matmul(PS[:, 7, k * P:TP], V[:, k, j * VD:(j + 1) * VD], PT[:, s * P:(s + w) * P],
                                         start=(k == 0), stop=(k == QT - 1))
                        s += w
                    last.then_inc(pv_done, 1)

                pe.wait_ge(qlat_evac, g * G + BEGUN)
                query_tiles(n, 0)
                pe.wait_ge(rope_evac, H // G)
                pe.wait_ge(o_done, g * G + BEGUN)
                query_tiles(n + 1, 1)
                pe.wait_ge(q_evac, g * G + 2)
                key_tiles(n + 2, 0)
                key_tiles(n + 3, 1)
                pe.wait_ge(qpe_ready, g + 1)
                scores(0)
                pe.wait_ge(q_evac, g * G + 4)
                value_tiles(n + 4, 0)
                value_tiles(n + 5, 1)
                for j in range(1, G):
                    scores(j)
                    turn_probs(j - 1)
                    values(j - 1)
                for j in range(G):
                    sample_queries(j)
                turn_probs(G - 1)
                values(G - 1)

            def sample_scores(b, first):
                pe.wait_ge(sq_ready, b + 1)
                pe.wait_ge(pgt_landed, b * (16 * NPG) + 16 * NPG)
                for c in range(3):
                    for k in range(CT):
                        pe.matmul(PS[:, c, 0:3 * P].rearrange("p (a n) -> p a n", a=3), QS[:, k * P:(k + 1) * P],
                                  PG[:, 3 * c:3 * c + 3, k * P:(k + 1) * P], start=(k == 0), stop=False)
                    last = pe.matmul(PS[:, c, 0:3 * P].rearrange("p (a n) -> p a n", a=3), QS[0:ROPE, CT * P:],
                                     PG[0:ROPE, 3 * c:3 * c + 3, CT * P:], start=False, stop=True)
                    last.then_inc(sqk_done, 1)
                if not first:
                    pe.wait_ge(olt_evac, b + (BEGUN - 1))
                for k in range(CT):
                    last = pe.transpose(PS[0:NS, 3, k * P:(k + 1) * P], PG[:, NPG, k * P:k * P + NS], ident)
                last.then_inc(new_done, 1)

            def sample_turn(b):
                pe.wait_ge(s_exp, b + 1)
                for j in range(NPG):
                    last = pe.transpose(PS[:, 4 + j // 4, (j % 4) * P:(j % 4 + 1) * P], PRS[:, j * P:(j + 1) * P], ident)
                    if j == 3:
                        last.then_inc(str_done, 1)
                last.then_inc(str_done, 1)
                pe.transpose(PS[0:NS, 6, 0:P], PRS[:, PAST:PAST + NS], ident).then_inc(str_done, 1)

            def sample_values(b, last=False):
                pe.wait_ge(spt_v, b * 2 + 2)
                pe.wait_ge(spt_a, b + 1)
                pe.wait_ge(new_evac, b + 1)
                if last:
                    pe.wait_ge(last_landed, 16 * NPG)
                else:
                    pe.wait_ge(nat_landed, b * (16 * NPG) + 16 * NPG)
                for j in range(NPG):
                    pe.matmul(PS[:, 7, :], PTS[:, j * P:(j + 1) * P], (NAT_LAST if last else NAT)[:, j, :], start=(j == 0), stop=False)
                pe.matmul(PS[:, 7, :], PTN[:, :], CKN[:, :], start=False, stop=True).then_inc(spv_done, 1)

            def sample_out_turn(b, new):
                pe.wait_ge(ols_ready, b + 1)
                pe.wait_ge(new_evac, new)
                for k in range(CT):
                    last = pe.transpose(PS[:, 3, k * P:(k + 1) * P], OLS[:, k * P:(k + 1) * P], ident)
                last.then_inc(olt_done, 1)

            pe.wait_ge(qlat_evac, H + BEGUN)
            pe.wait_ge(o_done, H + BEGUN)
            sample_scores(0, True)
            sample_turn(0)
            with pe.Fori(1, NB) as b:
                pe.wait_ge(s_exp, b)
                sample_scores(b, False)
                sample_values(b - 1)
                sample_turn(b)
                sample_out_turn(b - 1, b + 1)
            sample_values(NB - 1, last=True)
            pe.wait_ge(olt_evac, NB - 1 + BEGUN)
            sample_out_turn(NB - 1, NB)

            pe.wait_ge(olt_evac, NB + BEGUN)
            with pe.Fori(0, H // G) as i:
                for s in range(G):
                    pe.wait_ge(wv_landed[s], i * 16 + 16)
                    pe.wait_ge(so_evac, i * G + (s + 1 - G + SO_BEGUN))
                    for k in range(CT):
                        last = pe.matmul(PS[:, 4 + s, 0:P].rearrange("p (b t) -> p b t", b=NB), WV[:, s, k * VD:(k + 1) * VD],
                                         QLAT[:, k, :, bass.ds(i * (G * NS) + (s // 2) * (2 * NS), 2 * NS)],
                                         start=(k == 0), stop=(k == CT - 1))
                    last.then_inc(so_done, 1)

            project_out(W_OUT, o_ready, wo)

        @block.scalar
        def _(act):
            def round_w(n, width=CH):
                if n.i is not None or n.c >= 2:
                    act.wait_ge(w_used, n.at(-1))
                act.wait_ge(raw_landed[n.slot], n.turns() * 16)
                act.activation(WH[:, n.slot, 0:width], WR[:, n.slot, 0:width], ACT.Copy).then_inc(w_hi_ready, 1)

            def root(k, rows=T):
                act.wait_ge(var_ready, k)
                r = RS[(k - 1) % 2]
                act.activation(r[:, :], r[:, :], ACT.Sqrt).then_inc(root_ready, 1)

            for s in (*co["evac"], *wo["evac"], *qa_evac, *z1_evac):
                act.sem_inc(s, BEGUN)
            act.wait_ge(small_landed, 16)
            act.activation(small("c"), small("c"), ACT.Silu).then_inc(silu_c, 1)
            for k in range(KT):
                if k % 4 == 0:
                    act.wait_ge(x_landed[k // 4], 16)
                if k >= 2:
                    act.wait_ge(xsq_used[k % 2], k // 2)
                act.activation(TT[k % 2][:, :], X[:, k * T:(k + 1) * T], ACT.Square).then_inc(xsq_ready[k % 2], 1)
            root(1)

            def round_tiles(raw, hi_done, free=None):
                if free is not None:
                    act.wait_ge(w_used, free)
                for k in range(KT):
                    if raw is not None:
                        act.wait_ge(raw, k + 1)
                    act.activation(OH[:, k * T:(k + 1) * T], B1[:, k * T:(k + 1) * T], ACT.Copy).then_inc(hi_done, 1)

            for i in range(W_THREE):
                round_w(Chunk(i), CH3)
                for k in (2 * i, 2 * i + 1):
                    act.wait_ge(h_raw, k + 1)
                    act.activation(OH[:, k * T:(k + 1) * T], HX[:, k % 4 * T:(k % 4 + 1) * T], ACT.Copy).then_inc(h_hi, 1)
            round_w(Chunk(W_CONV - 2))
            round_w(Chunk(W_CONV - 1))
            act.activation(halves(T1[:, :]), pair(0), ACT.Copy).then_inc(c_ready, 1)
            act.activation(halves(T2[:, :]), pair(2), ACT.Silu).then_inc(z_ready, 1)
            round_w(Chunk(W_CONV))
            round_w(Chunk(W_CONV + 1))
            with act.Fori(1, KT) as m:
                n = Chunk(W_CONV - 8 + 2, 8, m)
                for k in range(8):
                    round_w(n + k)
                    if k == 1:
                        act.wait_ge(u_done, m)
                        act.activation(halves(T1[:, :]), pair(0), ACT.Copy).then_inc(c_ready, 1)
                    if k == 5:
                        act.wait_ge(gate_done, m)
                        act.activation(halves(T2[:, :]), pair(0), ACT.Silu).then_inc(z_ready, 1)

            act.wait_ge(gate_done, KT)
            round_tiles(None, y_hi, W_COUT)

            def project_out(w0, s, ahead):
                def body(i, n, split):
                    for j in range(2):
                        if split(j):
                            round_w(n + 2 * j)
                            round_w(n + (2 * j + 1))
                        else:
                            act.wait_ge(w_used, n.at(2 * j))
                        act.wait_ge(s["sq_used"][j], i + BEGUN)
                        act.activation(halves(TT[j][:, :]), pair(j), ACT.Square).then_inc(s["sq"][j], 1)
                        dst = B1[:, bass.ds(i * (2 * T) + j * T, T)]
                        act.activation(halves(dst), pair(j), ACT.Copy).then_inc(s["evac"][j], 1)
                last = KT // 2 if ahead else KT // 2 - 1
                with act.Fori(0, last) as i:
                    body(i, Chunk(w0 + 2, 4, i), lambda j: True)
                if not ahead:
                    body(KT // 2 - 1, Chunk(w0 + 2 + 4 * (KT // 2 - 1)), lambda j: j == 0)

            project_out(W_COUT, co, True)
            root(2)
            for k in range(KT):
                act.wait_ge(x1_ready, k + 1)
                if k >= 2:
                    act.wait_ge(x1sq_used[k % 2], k // 2)
                act.activation(TT[k % 2][:, :], X[:, k * T:(k + 1) * T], ACT.Square).then_inc(x1sq[k % 2], 1)
                act.activation(OH[:, k * T:(k + 1) * T], X[:, k * T:(k + 1) * T], ACT.Copy, scale=small("gin", k, 1)).then_inc(xg_hi, 1)
                if k % 2 and k >= 3:
                    round_w(Chunk(W_KV + k // 2 + 1))
            root(3)

            def h1_prompt(tiles):
                for k in tiles:
                    act.wait_ge(h1_normed, k + 1)
                    h = B1[:, k * T:k * T + TP]
                    act.activation(h, h, ACT.Identity, bias=MOD[:, 48 + k, 0:1], scale=AT[:, k, 0:1]).then_inc(h1_prompt_done, 1)

            for t in range(CT):
                if t < 3:
                    round_w(Chunk(W_KV + W_THREE + 1 + t))
                act.wait_ge(kv_evac, t + 1)
                if t >= 2:
                    act.wait_ge(kv_sq_used, t - 1 + BEGUN)
                act.activation(TT[t % 2][:, :], CKV[:, t * T:(t + 1) * T], ACT.Square).then_inc(kv_sq, 1)
                if t == 2:
                    h1_prompt(range(6))
            h1_prompt(range(6, KT - AHEAD))
            round_w(Chunk(W_MLA + 1))
            act.wait_ge(w_used, W_MLA)
            for k in range(KT):
                if k < AHEAD:
                    h1_prompt([KT - AHEAD + k])
                act.wait_ge(h1_raw, k + 1)
                act.wait_ge(h1_prompt_done, k + 1)
                act.activation(OH[:, k * T:(k + 1) * T], B1[:, k * T:(k + 1) * T], ACT.Copy).then_inc(h1_hi, 1)
            root(4)
            act.wait_ge(x_parked, 16)
            act.wait_ge(h1_raw, KT)
            with act.Fori(0, CT // 2) as i:
                n = Chunk(W_MLA + 2, 4, i)
                for j in range(2):
                    round_w(n + 2 * j)
                    round_w(n + (2 * j + 1))
                    act.wait_ge(qa_sq_used[j], i + BEGUN)
                    act.activation(halves(TT[j][:, :]), pair(j), ACT.Square).then_inc(qa_sq[j], 1)
                    act.activation(halves(QA[:, bass.ds(i * (2 * T) + j * T, T)]), pair(j), ACT.Copy).then_inc(qa_evac[j], 1)

            def gate_tiles(i, n):
                for j in range(2):
                    round_w(n + 2 * j)
                    round_w(n + (2 * j + 1))
                    dst = B1[:, bass.ds(i * (2 * T) + j * T, T)]
                    act.activation(halves(dst), pair(j), ACT.Silu).then_inc(z1_evac[j], 1)

            gate_tiles(0, Chunk(W_MLA + 2 * CT + 2))
            root(5)
            for k in range(CT):
                act.wait_ge(qn_raw, k + 1)
                act.activation(QNH[:, k * T:(k + 1) * T], QA[:, k * T:(k + 1) * T], ACT.Copy).then_inc(qn_hi, 1)
            with act.Fori(1, H // 2) as i:
                gate_tiles(i, Chunk(W_MLA + 2 * CT + 2, 4, i))
            act.wait_ge(ckv_ready, CT)
            for k in range(CT):
                act.activation(CKH[:, k * TP:(k + 1) * TP], CKV[:, k * T:k * T + TP], ACT.Copy).then_inc(ck_hi, 1)
            for g in range(H // G):
                round_w(Chunk(W_ROPE + 2 + g))

            with act.Fori(0, H // G) as g:
                n = Chunk(W_GRP + 2, 6, g)
                act.wait_ge(pv_done, g * G + BEGUN)
                for c in range(2):
                    round_w(n + c)
                    for jj in range(2):
                        act.activation(halves(QN[:, 2 * c + jj, :]), pair(2 * c + jj), ACT.Copy).then_inc(q_evac, 1)
                act.wait_ge(qn_ready, CT)
                act.wait_ge(qr_ready, H // G)
                act.activation(QPE[:, :], QPA[:, bass.ds(g * (2 * TP), 2 * TP)], ACT.Copy).then_inc(qpe_ready, 1)
                for c in range(2):
                    round_w(n + (2 + c))
                    for jj in range(2):
                        j = 2 * c + jj
                        act.activation(KTT[:, j * TP:(j + 1) * TP], PS[:, j, :], ACT.Copy).then_inc(k_evac, 1)

                def exps(j):
                    if j:
                        act.wait_ge(tr_done, g * 12 + 3 * j)
                    for i in range(QT):
                        o, w = P * (i * (i + 1) // 2), (i + 1) * P
                        act.wait_ge(bias_ready, g * 16 + (4 * j + i + 1))
                        act.activation(PR[:, o:o + w], PS[:, i, 0:w], ACT.Exp, bias=MX[:, 4 + i:5 + i],
                                       scale=SCALE, accum_out=MX[:, 8 + i:9 + i]).then_inc(exp_done, 1)

                def evac(j):
                    act.wait_ge(tr_done, g * 12 + (3 * j + 2))
                    act.activation(PT[:, 4 * P:8 * P], PS[:, 5, :], ACT.Copy).then_inc(pta_evac, 1)

                exps(0)
                for c in range(2):
                    round_w(n + (4 + c))
                for t in range(QT):
                    act.activation(V[:, t, :], PS[:, 4 + t, :], ACT.Copy).then_inc(v_evac, 1)
                for j in range(1, G):
                    evac(j - 1)
                    exps(j)
                evac(G - 1)

            def sample_exps(b, first):
                act.wait_ge(s_bias, b + 1)
                if not first:
                    act.wait_ge(str_done, b * 3)
                act.activation(PRS[:, 0:6 * P].rearrange("p (a n) -> p a n", a=2), PS[:, 0:2, 0:3 * P], ACT.Exp,
                               bias=MX[:, 4:5], scale=SCALE, accum_out=MX[:, 8:9])
                act.activation(PRS[:, 6 * P:PAST], PS[:, 2, 0:2 * P], ACT.Exp, bias=MX[:, 4:5], scale=SCALE,
                               accum_out=MX[:, 9:10])
                act.activation(PRS[:, PAST:PAST + NS], MX[:, 16:24], ACT.Exp, bias=MX[:, 4:5], scale=SCALE,
                               accum_out=MX[:, 10:11]).then_inc(s_exp, 1)

            def sample_probs(b):
                act.wait_ge(str_done, b * 3 + 2)
                act.activation(PTS[:, 4 * P:8 * P], PS[:, 5, :], ACT.Copy).then_inc(spt_a, 1)

            def sample_out(b):
                act.wait_ge(s_norm, b + 1)
                act.wait_ge(spv_done, b + 1)
                act.activation(OLS[:, :], PS[:, 7, :], ACT.Copy, scale=MX[:, 12:13]).then_inc(ols_ready, 1)

            sample_exps(0, True)
            sample_probs(0)
            with act.Fori(1, NB) as b:
                sample_exps(b, False)
                sample_out(b - 1)
                sample_probs(b)
            sample_out(NB - 1)

            act.wait_ge(so_evac, H + SO_BEGUN)
            round_tiles(None, o_hi)
            project_out(W_OUT, wo, False)
            root(6)

        @block.vector
        def _(dve):
            steps = [0, None]

            def step(ins):
                ins.then_inc(dve_step, 1)
                steps[0] += 1
                if steps[1] is None:
                    dve.wait_ge(dve_step, steps[0])
                else:
                    i, per, first = steps[1]
                    dve.wait_ge(dve_step, (i - first) * per + steps[0] if first else i * per + steps[0])

            def copy(out, in_):
                return dve.tensor_scalar(out, in_, 1.0, None, ALU.mult)

            def loop(first, end, per, body):
                before = steps[0]
                with dve.Fori(first, end) as i:
                    steps[1] = (i, per, first)
                    body(i)
                    assert steps[0] == before + per, (steps[0] - before, per)
                    steps[1] = None
                steps[0] = before + per * (end - first)

            def rstd(k, n, done=None):
                r = RS[(k - 1) % 2]
                dve.wait_ge(stat_done, k)
                dve.tensor_scalar(halves(r[:, :]), PS[:, 6:8, 0:HALF], 1.0 / n, EPS, ALU.mult, ALU.add).then_inc(var_ready, 1)
                dve.wait_ge(root_ready, k)
                if done is None:
                    step(dve.reciprocal(r[:, :], r[:, :]))
                else:
                    dve.reciprocal(r[:, :], r[:, :]).then_inc(done, 1)
                    dve.wait_ge(done, 1)

            def mod_part(n, bank, before):
                dve.wait_ge(ada_used, n * 4)
                if before is not None:
                    dve.wait_ge(ada_sel, before)
                dve.tensor_copy(PART[:, :], PS[:, bank, 0:AB]).then_inc(ada_part, 1)

            def mod_bias(n, bank, blk):
                dve.wait_ge(ada_sel, n)
                o = _C["bada"][0]
                dve.tensor_tensor(MOD[:, bass.ds(blk * 2, 2), :], PS[:, bank, 0:2 * NM].rearrange("p (a n) -> p a n", a=2),
                                  SM[:, bass.ds(blk * 2 + o, 2)].unsqueeze(2).broadcast_to([P, 2, NM]), ALU.add).then_inc(mod_done, 1)

            def scale_table(src, gain, one, k0=0, n=KT):
                gb = small(*gain, n).unsqueeze(2).broadcast_to([P, n, NM])
                step(dve.scalar_tensor_tensor(out=AT[:, k0:k0 + n, :], in0=MOD[:, src:src + n, :], scalar=one, in1=gb,
                                              op0=ALU.add, op1=ALU.mult))

            def modulate(tile, k, shift, raw, prompt=True):
                if prompt:
                    t = tile[:, 0:TP]
                    dve.tensor_scalar(t, t, AT[:, k, 0:1], MOD[:, shift + k, 0:1], ALU.mult, ALU.add)
                s = toks(tile[:, TP:T])
                step(dve.tensor_tensor(s, s, AT[:, k, 1:NM].unsqueeze(2).broadcast_to([P, NB, NS]), ALU.mult))
                dve.tensor_tensor(s, s, MOD[:, shift + k, 1:NM].unsqueeze(2).broadcast_to([P, NB, NS]), ALU.add).then_inc(raw, 1)

            def rest(k, hi_done, n, ready):
                dve.wait_ge(hi_done, n)
                c = slice(k * T, (k + 1) * T)
                dve.tensor_tensor(OL[:, c], B1[:, c], OH[:, c].bitcast(F32), ALU.subtract).then_inc(ready, 1)

            for s in (*co["sq_used"], *wo["sq_used"], *qa_sq_used, kv_sq_used, qlat_evac, o_done, olt_evac):
                dve.sem_inc(s, BEGUN)
            dve.sem_inc(so_evac, SO_BEGUN)
            rstd(1, D)
            dve.wait_ge(small_landed, 16)
            for q in range(4):
                dve.wait_ge(x_landed[q], 16)
            for i in range(ADA0 // 2):
                for q in range(2):
                    b = 2 * i + q
                    mod_part(b + 1, 6, b if b else None)
                    mod_bias(b + 1, 7, i + q * (ADA0 // 2))
                dve.wait_ge(mod_done, 2 * i + 2)
                scale_table(KT + 2 * i, ("gpre", 2 * i), 1.0, 2 * i, 2)
                for k in (2 * i, 2 * i + 1):
                    h = HX[:, k % 4 * T:(k % 4 + 1) * T]
                    if k >= 4:
                        dve.wait_ge(h_hi, k - 3)
                    step(dve.tensor_tensor(h, X[:, k * T:(k + 1) * T], R0[:, :], ALU.mult))
                    modulate(h, k, 0, h_raw)
                for k in (2 * i, 2 * i + 1):
                    c = slice(k * T, (k + 1) * T)
                    dve.wait_ge(h_hi, k + 1)
                    dve.tensor_tensor(OL[:, c], HX[:, k % 4 * T:(k % 4 + 1) * T], OH[:, c].bitcast(F32),
                                      ALU.subtract).then_inc(h_ready, 1)

            step(dve.memset(UP[:, 0:2], 0.0))

            def conv(m):
                a = m * 2 + ADA0
                mod_part(m * 2 + (ADA0 + 1), 6, a)
                dve.wait_ge(w_used, m * 8 + (W_CONV - 4))
                dve.wait_ge(c_ready, m + 1)
                so = _C["state"][0]
                copy(US[:, :, 0:2], SM[:, bass.ds(m * (2 * NB) + so, 2 * NB)].rearrange("p (b t) -> p b t", b=NB))
                dve.tensor_tensor(UP[:, 2:2 + HALF], PS[:, 2, 0:HALF], T1[:, 0:HALF], ALU.mult)
                dve.tensor_tensor(UP[:, 2 + HALF:2 + TP], PS[:, 3, 0:TP - HALF], T1[:, HALF:TP], ALU.mult)
                dve.tensor_tensor(US[:, :, 2:2 + NS], toks(PS[:, 3, TP - HALF:HALF]), toks(T1[:, TP:T]), ALU.mult).then_inc(u_done, 1)
                dve.wait_ge(u_done, m + 1)
                copy(CST[:, bass.ds(m * 18, 2)], UP[:, TP:TP + 2])
                copy(CST[:, bass.ds(m * 18 + 2, 16)].rearrange("p (b t) -> p b t", b=NB), US[:, :, NS:NS + 2])
                cs = toks(ACC[:, TP:T])
                for k in range(3):
                    w = SM[:, bass.ds(m * 3 + (_C["cw"][0] + k), 1)]
                    if k == 0:
                        dve.tensor_scalar(ACC[:, 0:TP], UP[:, 0:TP], w, None, ALU.mult)
                        step(dve.tensor_scalar(cs, US[:, :, 0:NS], w, None, ALU.mult))
                    else:
                        dve.scalar_tensor_tensor(out=ACC[:, 0:TP], in0=UP[:, k:k + TP], scalar=w, in1=ACC[:, 0:TP],
                                                 op0=ALU.mult, op1=ALU.add)
                        step(dve.scalar_tensor_tensor(out=cs, in0=US[:, :, k:k + NS], scalar=w, in1=cs,
                                                      op0=ALU.mult, op1=ALU.add))
                mod_bias(m * 2 + (ADA0 + 1), 7, a)
                mod_part(m * 2 + (ADA0 + 2), 6, m * 2 + (ADA0 + 1))
                dve.wait_ge(w_used, m * 8 + W_CONV)
                step(dve.tensor_tensor(halves(ACC[:, :]), pair(1), halves(ACC[:, :]), ALU.mult))
                dve.wait_ge(z_ready, m + 1)
                dve.tensor_tensor(B1[:, bass.ds(m * T, T)], ACC[:, :], T2[:, :], ALU.mult).then_inc(gate_done, 1)
                mod_bias(m * 2 + (ADA0 + 2), 7, m * 2 + (ADA0 + 1))

            loop(0, KT, 4, conv)
            dve.wait_ge(gate_done, KT)

            def project_out(hi_done, ready, s, layer):
                for t in range(KT):
                    rest(t, hi_done, t + 1, ready)
                scale_table(48 * layer + 2 * KT, ("gpost", KT * layer), 0.0)
                step(dve.memset(ACC[:, :], 0.0))

                def squares(i):
                    for j in range(2):
                        dve.wait_ge(s["sq"][j], i + 1)
                        dve.tensor_tensor(ACC[:, :], ACC[:, :], TT[j][:, :], ALU.add).then_inc(s["sq_used"][j], 1)
                        dve.wait_ge(s["evac"][j], i + 1 + BEGUN)
                        p = B1[:, bass.ds(i * (2 * T) + j * T, TP)]
                        dve.tensor_scalar(p, p, AT[:, bass.ds(i * 2 + j, 1), 0:1].rearrange("p a n -> p (a n)"), None, ALU.mult)
                        b = toks(B1[:, bass.ds(i * (2 * T) + (j * T + TP), TS)])
                        a = AT[:, bass.ds(i * 2 + j, 1), 1:NM].rearrange("p a n -> p (a n)").unsqueeze(2)
                        dve.tensor_tensor(b, b, a.broadcast_to([P, NB, NS]), ALU.mult).then_inc(s["scaled"][j], 1)
                        dve.wait_ge(s["sq_used"][j], i + 1 + BEGUN)
                loop(0, KT // 2, 0, squares)

            project_out(y_hi, y_ready, co, 0)

            def residual(r, which, s, before, ready, end=None):
                for j in range(2):
                    dve.wait_ge(s["scaled"][j], KT // 2)

                def add(n):
                    c = slice(which[n] * T, (which[n] + 1) * T)
                    dve.wait_ge(normed, before + n + 1)
                    dve.tensor_tensor(X[:, c], X[:, c], B1[:, c], ALU.add).then_inc(ready, 1)
                    if end:
                        end(n)

                for n, t in enumerate(which):
                    c = slice(t * T, (t + 1) * T)
                    dve.tensor_tensor(B1[:, c], B1[:, c], r[:, :], ALU.mult).then_inc(normed, 1)
                    if n:
                        add(n - 1)
                add(len(which) - 1)

            def rest_xg(t):
                if t:
                    c = slice((t - 1) * T, t * T)
                    dve.wait_ge(xg_hi, t)
                    dve.scalar_tensor_tensor(out=OL[:, c], in0=X[:, c], scalar=small("gin", t - 1, 1), in1=OH[:, c].bitcast(F32),
                                             op0=ALU.mult, op1=ALU.subtract).then_inc(xg_ready, 1)

            rstd(2, D)
            residual(R1, range(KT), co, 0, x1_ready, rest_xg)
            rest_xg(KT)
            scale_table(48 + KT, ("gpre", KT), 1.0)
            step(dve.memset(ACC[:, :], 0.0))
            rstd(3, D)
            def latent(t):
                dve.tensor_tensor(halves(CKV[:, t * T:(t + 1) * T]), pair(t), halves(R0[:, :]), ALU.mult).then_inc(kv_evac, 1)

            def latent_square(t):
                dve.wait_ge(kv_sq, t + 1)
                dve.tensor_tensor(ACC[:, :], ACC[:, :], TT[t % 2][:, :], ALU.add).then_inc(kv_sq_used, 1)
                dve.wait_ge(kv_sq_used, t + 1 + BEGUN)

            dve.wait_ge(w_used, W_KV + W_THREE)
            for t in range(3):
                latent(t)

            def h1(k):
                c = slice(k * T, (k + 1) * T)
                dve.tensor_tensor(B1[:, c], X[:, c], R0[:, :], ALU.mult).then_inc(h1_normed, 1)
                dve.wait_ge(h1_normed, k + 1)
                modulate(B1[:, c], k, 48, h1_raw, prompt=False)

            for k in range(KT - AHEAD):
                h1(k)
                if k < 3:
                    latent_square(k)
                if k == 6:
                    dve.wait_ge(w_used, W_KV + W_THREE + 2)
                    latent(3)
                if k == 8:
                    latent_square(3)
            dve.wait_ge(w_used, W_MLA)
            dve.wait_ge(rope_landed, 32)
            dve.tensor_tensor(halves(KPE[0:ROPE, :]), pair(2, ROPE), halves(R0[0:ROPE, :]), ALU.mult).then_inc(kv_evac, 1)
            dve.wait_ge(kv_evac, CT + 1)
            for k in range(KT):
                if k < AHEAD:
                    h1(KT - AHEAD + k)
                rest(k, h1_hi, k + 1, h1_ready)
            rstd(4, R)
            for t in range(CT):
                c = CKV[:, t * T:(t + 1) * T]
                dve.scalar_tensor_tensor(out=c, in0=c, scalar=small("glat", t, 1), in1=R1[:, :],
                                         op0=ALU.mult, op1=ALU.mult).then_inc(ckv_ready, 1)
            step(dve.tensor_tensor(ACC[0:RH, :], KPE[RH:ROPE, :], SIN[RH:ROPE, :], ALU.mult))
            step(dve.tensor_tensor(ACC[RH:ROPE, :], KPE[0:RH, :], SIN[0:RH, :], ALU.mult))
            step(dve.tensor_tensor(KPE[0:ROPE, :], KPE[0:ROPE, :], COS[0:ROPE, :], ALU.mult))
            step(dve.tensor_tensor(KPE[0:RH, :], KPE[0:RH, :], ACC[0:RH, :], ALU.subtract))
            step(dve.tensor_tensor(KPE[RH:ROPE, :], KPE[RH:ROPE, :], ACC[RH:ROPE, :], ALU.add))
            dve.tensor_copy(KPE[ROPE:P, 0:TP], KPE[0:ROPE, 0:TP]).then_inc(kpe_ready, 1)
            step(dve.memset(ACC[:, :], 0.0))

            def qa_squares(i):
                for j in range(2):
                    dve.wait_ge(qa_sq[j], i + 1)
                    dve.tensor_tensor(ACC[:, :], ACC[:, :], TT[j][:, :], ALU.add).then_inc(qa_sq_used[j], 1)
                    dve.wait_ge(qa_sq_used[j], i + 1 + BEGUN)

            loop(0, CT // 2, 0, qa_squares)
            rstd(5, R)
            for j in range(2):
                dve.wait_ge(qa_evac[j], CT // 2 + BEGUN)
            for k in range(CT):
                c = QA[:, k * T:(k + 1) * T]
                dve.scalar_tensor_tensor(out=c, in0=c, scalar=small("gq", k, 1), in1=R0[:, :],
                                         op0=ALU.mult, op1=ALU.mult).then_inc(qn_raw, 1)
            for k in range(CT):
                c = slice(k * T, (k + 1) * T)
                dve.wait_ge(qn_hi, k + 1)
                dve.tensor_tensor(QNL[:, c], QA[:, c], QNH[:, c].bitcast(F32), ALU.subtract).then_inc(qn_ready, 1)
            for k in range(CT):
                dve.wait_ge(ck_hi, k + 1)
                dve.tensor_tensor(CKL[:, k * TP:(k + 1) * TP], CKV[:, k * T:k * T + TP],
                                  CKH[:, k * TP:(k + 1) * TP].bitcast(F32), ALU.subtract).then_inc(ck_ready, 1)
            for g in range(H // G):
                dve.wait_ge(w_used, W_ROPE + g + 1)
                for dst, p, tab in ((T1, 0, COS), (T2, 1, SIN), (ACC, 1, COS)):
                    dve.tensor_tensor(halves(dst[:, :]), pair(2 * (g % 2) + p), halves(tab[:, :]), ALU.mult)
                dve.tensor_tensor(halves(R1[:, :]), pair(2 * (g % 2)), halves(SIN[:, :]), ALU.mult).then_inc(rope_evac, 1)
                dve.wait_ge(rope_evac, g + 1)
                for j in range(G):
                    s = slice(RH * j, RH * j + RH)
                    r, c = ROPE * (j % 2), (2 * g + j // 2) * TP
                    dve.tensor_tensor(QPA[r:r + RH, c:c + TP], T1[s, 0:TP], T2[s, 0:TP], ALU.subtract)
                    dve.tensor_tensor(QPA[r + RH:r + ROPE, c:c + TP], ACC[s, 0:TP], R1[s, 0:TP], ALU.add)
                    dve.tensor_tensor(QPS[0:RH, :, G * g + j, :], toks(T1[s, TP:T]), toks(T2[s, TP:T]), ALU.subtract)
                    last = dve.tensor_tensor(QPS[RH:ROPE, :, G * g + j, :], toks(ACC[s, TP:T]), toks(R1[s, TP:T]), ALU.add)
                last.then_inc(qr_ready, 1)
                dve.wait_ge(qr_ready, g + 1)

            def group(g):
                def maxima(j):
                    for i in range(QT):
                        dve.wait_ge(score_done, g * 16 + (4 * j + i + 1))
                        if j:
                            dve.wait_ge(exp_done, g * 16 + (4 * (j - 1) + i + 1))
                        d = PS[:, i, i * P:(i + 1) * P]
                        step(dve.tensor_tensor(d, d, small("mask"), ALU.add))
                        step(dve.tensor_reduce(MX[:, i:i + 1], PS[:, i, 0:(i + 1) * P], AX.X, ALU.max))
                        dve.tensor_scalar(MX[:, 4 + i:5 + i], MX[:, i:i + 1], -SCALE, None, ALU.mult).then_inc(bias_ready, 1)

                def normalise(j):
                    for i in range(QT):
                        o, w = P * (i * (i + 1) // 2), (i + 1) * P
                        dve.wait_ge(exp_done, g * 16 + (4 * j + i + 1))
                        step(dve.reciprocal(MX[:, 12 + i:13 + i], MX[:, 8 + i:9 + i]))
                        last = dve.tensor_scalar(PR[:, o:o + w], PR[:, o:o + w], MX[:, 12 + i:13 + i], None, ALU.mult)
                    last.then_inc(p_ready, 1)

                def turned(j):
                    dve.wait_ge(tr_done, g * 12 + (3 * j + 1))
                    dve.tensor_copy(PT[:, 0:4 * P], PS[:, 4, :]).then_inc(ptv_evac, 1)
                    dve.wait_ge(tr_done, g * 12 + (3 * j + 3))
                    dve.tensor_copy(PT[:, 8 * P:10 * P], PS[:, 6, 0:2 * P]).then_inc(ptv_evac, 1)

                def out(j):
                    dve.wait_ge(pv_done, g * G + (j + 1 + BEGUN))
                    o = B1[:, bass.ds(g * (G * T) + j * T, TP)]
                    dve.tensor_tensor(o, PS[:, 7, :], o, ALU.mult).then_inc(o_done, 1)

                maxima(0)
                normalise(0)
                for j in range(1, G):
                    maxima(j)
                    turned(j - 1)
                    normalise(j)
                    out(j - 1)
                for j in range(G):
                    dve.wait_ge(qlat_done, g * G + (j + 1))
                    dst = QLAT[:, :, :, bass.ds(g * (G * NS) + j * NS, NS)]
                    src = PS[:, j, :].rearrange("p (k n) -> p k n", k=CT)[:, :, TS:P]
                    copy(dst, src.rearrange("p k (b t) -> p k b t", b=NB)).then_inc(qlat_evac, 1)
                turned(G - 1)
                out(G - 1)

            for j in range(2):
                dve.wait_ge(z1_evac[j], H // 2 + BEGUN)
            loop(0, H // G, G * QT * 3, group)

            step(dve.memset(PG[:, NPG, :], 0.0))

            def sample_prepare(b, first):
                if not first:
                    dve.wait_ge(new_done, b)
                copy(QS[:, 0:CT * P].rearrange("p (k n) -> p k n", k=CT), QLAT[:, :, bass.ds(b, 1), :].rearrange("p k a n -> p k (a n)"))
                copy(QS[0:ROPE, CT * P:], QPS[:, bass.ds(b, 1), :, :].rearrange("p a h t -> p (a h t)"))
                copy(PG[0:ROPE, NPG, CT * P:CT * P + NS], KPE[0:ROPE, bass.ds(b * NS + TP, NS)])
                copy(PG[:, NPG, 0:CT * P].rearrange("p (k n) -> p k n", k=CT)[:, :, 0:NS],
                     CKV[:, :].rearrange("p (k n) -> p k n", k=CT)[:, :, bass.ds(b * NS + TP, NS)]).then_inc(sq_ready, 1)

            def sample_maxima(b):
                dve.wait_ge(sqk_done, b * 3 + 3)
                step(dve.tensor_tensor(MX[:, 16:24], PS[:, 2, 2 * P:2 * P + NS], small("mask8"), ALU.add))
                dve.tensor_reduce(MX[:, 0:1], PS[:, 0:2, 0:3 * P], AX.XY, ALU.max)
                dve.tensor_reduce(MX[:, 1:2], PS[:, 2, 0:2 * P], AX.X, ALU.max)
                step(dve.tensor_reduce(MX[:, 2:3], MX[:, 16:24], AX.X, ALU.max))
                step(dve.tensor_reduce(MX[:, 3:4], MX[:, 0:3], AX.X, ALU.max))
                dve.tensor_scalar(MX[:, 4:5], MX[:, 3:4], -SCALE, None, ALU.mult).then_inc(s_bias, 1)

            def sample_new(b, first):
                dve.wait_ge(new_done, b + 1)
                if not first:
                    dve.wait_ge(spv_done, b)
                dve.tensor_copy(CKN[:, :], PS[0:NS, 3, :]).then_inc(new_evac, 1)

            def sample_probs(b, first):
                dve.wait_ge(s_exp, b + 1)
                step(dve.tensor_reduce(MX[:, 11:12], MX[:, 8:11], AX.X, ALU.add))
                if not first:
                    dve.wait_ge(ols_ready, b)
                dve.reciprocal(MX[:, 12:13], MX[:, 11:12]).then_inc(s_norm, 1)
                dve.wait_ge(str_done, b * 3 + 1)
                dve.tensor_copy(PTS[:, 0:4 * P], PS[:, 4, :]).then_inc(spt_v, 1)
                dve.wait_ge(str_done, b * 3 + 3)
                dve.tensor_copy(PTN[:, :], PS[0:NS, 6, 0:P]).then_inc(spt_v, 1)

            def sample_out(b):
                dve.wait_ge(olt_done, b + 1)
                copy(QLAT[:, :, bass.ds(b, 1), :].rearrange("p k a n -> p k (a n)"),
                     PS[:, 3, :].rearrange("p (k n) -> p k n", k=CT)).then_inc(olt_evac, 1)

            def batch(b, last=False):
                sample_maxima(b)
                sample_new(b, False)
                if not last:
                    sample_prepare(b + 1, False)
                sample_probs(b, False)
                sample_out(b - 1)

            sample_prepare(0, True)
            sample_maxima(0)
            sample_new(0, True)
            sample_prepare(1, False)
            sample_probs(0, True)
            loop(1, NB - 1, 4, batch)
            batch(NB - 1, True)
            sample_out(NB - 1)

            def sample_gate(i):
                for s in range(G):
                    dve.wait_ge(so_done, i * G + (s + 1))
                    o = toks(B1[:, bass.ds(i * (G * T) + (s * T + TP), TS)])
                    mine = toks(PS[:, 4 + s, 0:P])[:, :, s % 2 * NS:(s % 2 + 1) * NS]
                    dve.tensor_tensor(o, mine, o, ALU.mult).then_inc(so_evac, 1)

            loop(0, H // G, 0, sample_gate)
            dve.wait_ge(so_evac, H + SO_BEGUN)
            project_out(o_hi, o_ready, wo, 1)
            rstd(6, D, out_rstd)
            dve.wait_ge(x1_back, 16)
            residual(R1, [t for t in range(KT) if t not in ON_POOL], wo, KT, yout_ready)


def kernel(x_prompt, x_sample, state_conv, cache_ckv, cache_kpe, page_table, c_prompt, c_sample,
           w_ada, b_ada, g_pre, g_post, conv_w_in, conv_w, conv_w_out,
           kv_g_in, kv_w_down, kv_g_latent, kv_w_up, mla_w_in, mla_g_q, mla_w_uq, mla_w_out):
    import concourse.bacc as bacc
    from concourse.bass_utils import run_bass_kernel_spmd

    f = lambda a: np.asarray(a)
    (x_prompt, x_sample, state_conv, cache_ckv, cache_kpe, page_table, c_prompt, c_sample, w_ada, b_ada, g_pre,
     g_post, conv_w_in, conv_w, conv_w_out, kv_g_in, kv_w_down, kv_g_latent, kv_w_up, mla_w_in, mla_g_q, mla_w_uq,
     mla_w_out) = map(f, (x_prompt, x_sample, state_conv, cache_ckv, cache_kpe, page_table, c_prompt, c_sample,
                          w_ada, b_ada, g_pre, g_post, conv_w_in, conv_w, conv_w_out, kv_g_in, kv_w_down,
                          kv_g_latent, kv_w_up, mla_w_in, mla_g_q, mla_w_uq, mla_w_out))

    def tiles(a):
        return a.reshape(-1, P, a.shape[-1]).transpose(1, 0, 2).reshape(P, -1)

    def chunks(w, kts, cols):
        k, n = w.shape
        a = w.reshape(k // (kts * P), kts, P, n // cols, cols).transpose(3, 0, 2, 1, 4)
        return a.reshape(-1, P, kts * cols)

    def three(w):
        a = chunks(w, 2, 3 * P)
        return np.concatenate([a, np.zeros(a.shape[:2] + (CH - CH3,), a.dtype)], axis=2)

    x = np.concatenate([x_prompt[0].T, x_sample.reshape(TS, D).T], axis=1)
    w_in = conv_w_in[0].reshape(D, 4, KT, P)[:, [1, 2, 3, 0]].transpose(0, 2, 1, 3).reshape(D, -1)
    uq = mla_w_uq[0].reshape(R, H, NOPE + ROPE)
    nope = uq[:, :, :NOPE].reshape(R, -1)
    rope = uq[:, :, NOPE:].reshape(R, H // G, G, 2, RH).transpose(0, 1, 3, 2, 4).reshape(R, -1)
    up_k = kv_w_up[:, :, :NOPE].reshape(R, -1)
    up_v = kv_w_up[:, :, NOPE:].reshape(R, -1)
    k_chunks = chunks(up_k, CT, 256).reshape(H // G, 2, P, CH)
    v_chunks = chunks(up_v, 2, 512).reshape(H // G, 2, P, CH)
    q_chunks = chunks(nope, CT, 256).reshape(H // G, 2, P, CH)
    groups = np.concatenate([q_chunks, k_chunks, v_chunks], axis=1).reshape(-1, P, CH)
    wstream = np.concatenate([
        three(w_in[:, :3 * P]), chunks(w_in[:, 3 * P:], 8, P), chunks(conv_w_out[0], 8, P),
        three(kv_w_down[:, :3 * P]), chunks(kv_w_down[:, 3 * P:R], 8, P),
        chunks(kv_w_down[:, R:], KT, ROPE), chunks(mla_w_in[0], 8, P), chunks(rope, CT, 256), groups,
        chunks(mla_w_out[0], 8, P)])
    assert wstream.shape[0] == W_END
    ada = np.concatenate([w_ada[0], w_ada[1]], axis=1)
    adastream = ada.reshape(4, 4, P, 48, AB).transpose(3, 0, 2, 1, 4).reshape(48, 4, P, CH)
    c = np.concatenate([c_prompt, c_sample], axis=0)
    cpad = np.concatenate([c.T, np.zeros((D, 32 - NM), np.float32)], axis=1)
    sel = np.zeros((P, NM), np.float32)
    for r in range(NM):
        sel[r::32, r] = 1.0
    q, k = np.arange(P)[:, None], np.arange(P)[None, :]
    mask = np.where(k <= q, 0.0, NEG).astype(np.float32)
    mask8 = np.where(np.arange(NS)[None, :] <= (np.arange(P) % NS)[:, None], 0.0, NEG).astype(np.float32)
    col = lambda a: a.reshape(-1, P).T
    small_in = np.concatenate([
        col(b_ada), col(g_pre), col(g_post), col(kv_g_in), col(kv_g_latent), col(mla_g_q),
        tiles(np.ascontiguousarray(conv_w[0].T)), tiles(cpad),
        tiles(state_conv[0].transpose(2, 0, 1).reshape(D, -1)),
        np.eye(P, dtype=np.float32), np.ones((P, P), np.float32), sel, mask, mask8], axis=1)
    assert small_in.shape == (P, SMALL)
    pos = np.concatenate([np.arange(TP), np.tile(PAST + np.arange(NS), NB)]).astype(np.float32)
    inv = (np.float32(10000.0) ** (-np.arange(RH, dtype=np.float32) / np.float32(RH))).astype(np.float32)
    ang = (pos[None, :] * inv[:, None]).astype(np.float32).astype(np.float64)
    cos_in = np.tile(np.cos(ang).astype(np.float32), (4, 1))
    sin_in = np.tile(np.sin(ang).astype(np.float32), (4, 1))
    ct = cache_ckv.reshape(POOL_PAGES, PAGE, CT, P).transpose(0, 3, 2, 1).reshape(POOL_PAGES, P, -1)
    kp = np.concatenate([cache_kpe.transpose(0, 2, 1), np.zeros((POOL_PAGES, P - ROPE, PAGE), np.float32)], axis=1)
    pages = np.concatenate([ct, kp, cache_ckv], axis=2)
    wk = kv_w_up[:, :, :NOPE].transpose(1, 2, 0)
    wv = kv_w_up[:, :, NOPE:].reshape(CT, P, H, VD).transpose(2, 1, 0, 3).reshape(H, P, -1)

    ins = {"wstream": wstream, "adastream": adastream, "x_in": tiles(x), "small_in": small_in, "cos_in": cos_in,
           "sin_in": sin_in, "pages": pages, "ptab": page_table.reshape(1, -1).astype(np.int32), "wk_in": wk, "wv_in": wv}
    ins = {k: np.ascontiguousarray(v) for k, v in ins.items()}
    nc = bacc.Bacc("TRN2", target_bir_lowering=False, num_devices=1)
    args = {k: nc.dram_tensor(k, v.shape, mybir.dt.from_np(v.dtype), kind="ExternalInput").ap() for k, v in ins.items()}
    outs = {"y_out": (P, KT * T), "cst_out": (P, KT * 18), "ckv_out": (P, CT * T), "kpe_out": (ROPE, T)}
    for k, s in outs.items():
        args[k] = nc.dram_tensor(k, s, F32, kind="ExternalOutput").ap()
    args["x1_park"] = nc.dram_tensor("x1_park", (P, KT * T), F32, kind="Internal").ap()
    build(nc, **args)
    r = run_bass_kernel_spmd(nc, [ins], core_ids=[0]).results[0]

    def rows(a):
        return a.reshape(P, -1, T).transpose(2, 1, 0).reshape(T, -1)

    y, ckv, kpe = rows(r["y_out"]), rows(r["ckv_out"]), r["kpe_out"].T
    cst = r["cst_out"].reshape(P, KT, 18).transpose(2, 1, 0).reshape(18, D)
    c_ = np.ascontiguousarray
    return (c_(y[:TP])[None], c_(y[TP:]).reshape(NB, NS, D), c_(cst[:2])[None, None],
            c_(cst[2:]).reshape(1, NB, 2, D), c_(ckv[:TP])[None], c_(kpe[:TP])[None],
            c_(ckv[TP:]).reshape(NB, NS, R), c_(kpe[TP:]).reshape(NB, NS, ROPE))
```
